# Optimizing a Trainium2 kernel written in Bass

```python
import math
import jax
import jax.numpy as jnp
from jax import lax
import numpy as np

D_MODEL = 1024
BATCH = 1
SEQ = 512
DEPTH = 2
DEC_BATCH = 8
DEC_SEQ = 8
PAST_LEN = 256
PAGE_SIZE = 128

HEAD_DIM = 64
CONV_K = 4
RMS_EPS = 1e-6
MLP_HIDDEN = 4 * D_MODEL
QUERY_BLOCK = 128
N_AB = (DEPTH + 1) // 2
N_CD = DEPTH // 2

SSM_HEADS = D_MODEL // 64
SSM_HEAD_DIM = 64
SSM_INNER = SSM_HEADS * SSM_HEAD_DIM
SSM_GROUPS = 2
SSM_STATE = 128
SSM_CONV_DIM = SSM_INNER + 2 * SSM_GROUPS * SSM_STATE
SSM_CHUNK = 128

NSA_HEADS = D_MODEL // 64
NSA_KV_HEADS = 2
NSA_REP = NSA_HEADS // NSA_KV_HEADS
NSA_BLOCK = 64
NSA_TOPK = 16
NSA_WINDOW = 512
NSA_CMP_HIDDEN = 256

GDN_HEADS = D_MODEL // 128
GDN_HEAD_DIM = 128
GDN_WIDTH = GDN_HEADS * GDN_HEAD_DIM
GDN_CHUNK = 64

DIL_PATTERNS = ((128, 1), (512, 4), (2048, 16))
DIL_GROUPS = len(DIL_PATTERNS)
DIL_HEADS_PER_GROUP = 8

AB_IN = SSM_INNER + SSM_CONV_DIM + SSM_HEADS + NSA_HEADS * HEAD_DIM + 6 * NSA_KV_HEADS * HEAD_DIM + 3 * NSA_HEADS
AB_MIX = SSM_INNER + NSA_HEADS * HEAD_DIM
DIL_IN = 3 * DIL_GROUPS * DIL_HEADS_PER_GROUP * HEAD_DIM
CD_IN = 4 * GDN_WIDTH + 2 * GDN_HEADS + DIL_IN
CD_MIX = GDN_WIDTH + DIL_HEADS_PER_GROUP * HEAD_DIM
NEG = -1e30

kernel_name = 'hybrid_ssd_nsa_gdn_dilated_decoder_step'

def split_cols(x, sizes):
    cuts, acc = [], 0
    for s in sizes[:-1]:
        acc += s
        cuts.append(acc)
    return jnp.split(x, cuts, axis=-1)

def rmsnorm(x, w):
    xf = x.astype(jnp.float32)
    y = xf * lax.rsqrt(jnp.mean(xf * xf, axis=-1, keepdims=True) + RMS_EPS)
    return (y * w.astype(jnp.float32)).astype(x.dtype)

def l2norm(x):
    xf = x.astype(jnp.float32)
    return xf * lax.rsqrt(jnp.sum(xf * xf, axis=-1, keepdims=True) + 1e-6)

def causal_conv(x, buf, w, b):
    t = x.shape[1]
    xp = jnp.concatenate([buf.astype(x.dtype), x], axis=1)
    y = xp[:, 0:t] * w[0]
    for i in range(1, CONV_K):
        y = y + xp[:, i:i + t] * w[i]
    if b is not None:
        y = y + b
    return y, xp[:, t:]

def attend_dense(q, k, v, mask):
    s = jnp.einsum('bqgrd,bkgd->bqgrk', q, k).astype(jnp.float32) * (q.shape[-1] ** -0.5)
    s = jnp.where(mask[:, :, None, None, :], s, NEG)
    m = jnp.max(s, axis=-1, keepdims=True)
    p = jnp.exp(s - m)
    l = jnp.sum(p, axis=-1, keepdims=True)
    o = jnp.einsum('bqgrk,bkgd->bqgrd', (p / l).astype(v.dtype), v)
    return o, (m + jnp.log(l))[..., 0]

def attend_gathered(q, k, v, mask):
    s = jnp.einsum('bqgrd,bqgkd->bqgrk', q, k).astype(jnp.float32) * (q.shape[-1] ** -0.5)
    s = jnp.where(mask[:, :, :, None, :], s, NEG)
    m = jnp.max(s, axis=-1, keepdims=True)
    p = jnp.exp(s - m)
    l = jnp.sum(p, axis=-1, keepdims=True)
    o = jnp.einsum('bqgrk,bqgkd->bqgrd', (p / l).astype(v.dtype), v)
    return o, (m + jnp.log(l))[..., 0]

def banded_attention(q, k, v, window, qblk):
    bsz, t, g, r, hd = q.shape
    nq = t // qblk
    span = qblk + window
    kp = jnp.pad(k, ((0, 0), (window, 0), (0, 0), (0, 0)))
    vp = jnp.pad(v, ((0, 0), (window, 0), (0, 0), (0, 0)))
    diff = jnp.arange(qblk)[:, None] - jnp.arange(span)[None, :] + window
    band = (diff >= 0) & (diff <= window)

    def one(args):
        i, qi = args
        start = i * qblk
        ks = lax.dynamic_slice_in_dim(kp, start, span, axis=1)
        vs = lax.dynamic_slice_in_dim(vp, start, span, axis=1)
        kpos = start + jnp.arange(span) - window
        return attend_dense(qi, ks, vs, (band & (kpos >= 0)[None, :])[None])

    qs = q.reshape(bsz, nq, qblk, g, r, hd).swapaxes(0, 1)
    o, lse = lax.map(one, (jnp.arange(nq), qs))
    return o.swapaxes(0, 1).reshape(bsz, t, g, r, hd), lse.swapaxes(0, 1).reshape(bsz, t, g, r)

def ssd_scan(x, dt, a, bm, cm, h0, chunk):
    bsz, t, nh, hp = x.shape
    ng, ns = bm.shape[2], bm.shape[3]
    rep = nh // ng
    nc = t // chunk
    f32 = jnp.float32
    la = (dt * a).reshape(bsz, nc, chunk, ng, rep)
    xd = (x.astype(f32) * dt[..., None]).reshape(bsz, nc, chunk, ng, rep, hp)
    bc = bm.astype(f32).reshape(bsz, nc, chunk, ng, ns)
    cc = cm.astype(f32).reshape(bsz, nc, chunk, ng, ns)
    acs = jnp.cumsum(la, axis=2)
    ii = jnp.arange(chunk)
    incl = ii[:, None] >= ii[None, :]
    lmat = jnp.exp(jnp.where(incl[:, :, None, None], acs[:, :, :, None] - acs[:, :, None, :], -jnp.inf))
    cb = jnp.einsum('bcign,bcjgn->bcijg', cc, bc)
    y_diag = jnp.einsum('bcijgr,bcjgrp->bcigrp', cb[..., None] * lmat, xd)
    states = jnp.einsum('bcjgn,bcjgrp->bcgrpn', bc, xd * jnp.exp(acs[:, :, -1:] - acs)[..., None])
    cdec = jnp.exp(acs[:, :, -1])

    def step(h, inp):
        s, d = inp
        return d[..., None, None] * h + s, h

    h_fin, h_prev = lax.scan(step, h0.astype(f32).reshape(bsz, ng, rep, hp, ns),
                             (jnp.moveaxis(states, 1, 0), jnp.moveaxis(cdec, 1, 0)))
    h_prev = jnp.moveaxis(h_prev, 0, 1)
    y_off = jnp.einsum('bcign,bcgrpn->bcigrp', cc, h_prev) * jnp.exp(acs)[..., None]
    return (y_diag + y_off).reshape(bsz, t, nh, hp), h_fin.reshape(bsz, nh, hp, ns)

def gated_delta(q, k, v, g, beta, s0, chunk):
    bsz, t, nh, dk = q.shape
    dv = v.shape[-1]
    nc = t // chunk
    f32 = jnp.float32

    def rs(arr):
        return arr.astype(f32).reshape((bsz, nc, chunk) + arr.shape[2:])

    q, k, v, beta = rs(q), rs(k), rs(v), rs(beta)
    gc = jnp.cumsum(rs(g), axis=2)
    kb = k * beta[..., None]
    vb = v * beta[..., None]
    ii = jnp.arange(chunk)
    incl = ii[:, None] >= ii[None, :]
    strict = ii[:, None] > ii[None, :]
    decay = jnp.exp(jnp.where(incl[:, :, None], gc[:, :, :, None, :] - gc[:, :, None, :, :], -jnp.inf))
    amat = jnp.where(strict[:, :, None], jnp.einsum('bcihk,bcjhk->bcijh', kb, k) * decay, 0.0)
    amat = jnp.moveaxis(amat, -1, 2)
    eye = jnp.eye(chunk, dtype=f32)
    tmat = lax.linalg.triangular_solve(amat + eye, jnp.broadcast_to(eye, amat.shape),
                                       left_side=True, lower=True, unit_diagonal=True)
    u = jnp.einsum('bchij,bcjhv->bcihv', tmat, vb)
    w = jnp.einsum('bchij,bcjhk->bcihk', tmat, kb * jnp.exp(gc)[..., None])
    qk = jnp.where(incl[:, :, None], jnp.einsum('bcihk,bcjhk->bcijh', q, k) * decay, 0.0)
    qg = q * jnp.exp(gc)[..., None]
    kdec = k * jnp.exp(gc[:, :, -1:] - gc)[..., None]
    glast = jnp.exp(gc[:, :, -1])

    def step(s, inp):
        qg_c, kdec_c, u_c, w_c, qk_c, gl = inp
        v_new = u_c - jnp.einsum('bihk,bhkv->bihv', w_c, s)
        o = jnp.einsum('bihk,bhkv->bihv', qg_c, s) + jnp.einsum('bijh,bjhv->bihv', qk_c, v_new)
        s = s * gl[:, :, None, None] + jnp.einsum('bjhk,bjhv->bhkv', kdec_c, v_new)
        return s, o

    xs = tuple(jnp.moveaxis(arr, 1, 0) for arr in (qg, kdec, u, w, qk, glast))
    s_fin, o = lax.scan(step, s0.astype(f32), xs)
    return jnp.moveaxis(o, 0, 1).reshape(bsz, t, nh, dv), s_fin

def compress_blocks(k, pe, w1, w2):
    bsz, length, g, hd = k.shape
    nb = length // NSA_BLOCK
    kb = k.reshape(bsz, nb, NSA_BLOCK, g, hd) + pe[:, None, :]
    flat = kb.transpose(0, 1, 3, 2, 4).reshape(bsz, nb, g, NSA_BLOCK * hd)
    return jax.nn.silu(flat @ w1) @ w2

def nsa_global(q, k_cmp, v_cmp, k_sel, v_sel, q_pos, lp, qblk):
    bsz, tq, g, r, hd = q.shape
    length = k_cmp.shape[1]
    nb = -(-length // NSA_BLOCK)
    pad = ((0, 0), (0, nb * NSA_BLOCK - length), (0, 0), (0, 0))
    kc = compress_blocks(jnp.pad(k_cmp, pad), lp['nsa_pe_k'], lp['nsa_ck_w1'], lp['nsa_ck_w2'])
    vc = compress_blocks(jnp.pad(v_cmp, pad), lp['nsa_pe_v'], lp['nsa_cv_w1'], lp['nsa_cv_w2'])
    kb = jnp.pad(k_sel, pad).reshape(bsz, nb, NSA_BLOCK, g, hd).transpose(0, 3, 1, 2, 4)
    vb = jnp.pad(v_sel, pad).reshape(bsz, nb, NSA_BLOCK, g, hd).transpose(0, 3, 1, 2, 4)
    n_sel = min(NSA_TOPK, nb)
    blk = jnp.arange(nb)
    b_idx = jnp.arange(bsz)[:, None, None, None]
    g_idx = jnp.arange(g)[None, None, :, None]
    scale = hd ** -0.5

    def one(args):
        qi, pos = args
        cur = pos // NSA_BLOCK
        complete = (blk[None, :] + 1) * NSA_BLOCK <= pos[:, None] + 1
        s = jnp.einsum('bqgrd,bngd->bqgrn', qi, kc).astype(jnp.float32) * scale
        s = jnp.where(complete[None, :, None, None, :], s, NEG)
        p = jax.nn.softmax(s, axis=-1)
        p = jnp.where(jnp.any(complete, axis=-1)[None, :, None, None, None], p, 0.0)
        o_cmp = jnp.einsum('bqgrn,bngd->bqgrd', p.astype(vc.dtype), vc)
        imp = jnp.sum(p, axis=3)
        forced = (blk[None, :] == 0) | (blk[None, :] == cur[:, None]) | (blk[None, :] == cur[:, None] - 1)
        future = blk[None, :] > cur[:, None]
        score = jnp.where(forced[None, :, None, :], r + 1.0, imp)
        score = jnp.where(future[None, :, None, :], -1.0, score)
        _, sel = lax.top_k(score, n_sel)
        qb = qi.shape[1]
        ks = kb[b_idx, g_idx, sel].reshape(bsz, qb, g, n_sel * NSA_BLOCK, hd)
        vs = vb[b_idx, g_idx, sel].reshape(bsz, qb, g, n_sel * NSA_BLOCK, hd)
        kpos = sel[..., None] * NSA_BLOCK + jnp.arange(NSA_BLOCK)
        valid = (kpos <= pos[None, :, None, None, None]).reshape(bsz, qb, g, n_sel * NSA_BLOCK)
        o_sel, _ = attend_gathered(qi, ks, vs, valid)
        return o_cmp, o_sel

    nq = tq // qblk
    qs = q.reshape(bsz, nq, qblk, g, r, hd).swapaxes(0, 1)
    o_cmp, o_sel = lax.map(one, (qs, q_pos.reshape(nq, qblk)))
    return (o_cmp.swapaxes(0, 1).reshape(bsz, tq, g, r, hd),
            o_sel.swapaxes(0, 1).reshape(bsz, tq, g, r, hd))

def dilated_prompt(q, k, v, win, dil):
    bsz, t, nh, hd = q.shape
    n = t // dil

    def to_cls(arr):
        return arr.reshape(bsz, n, dil, nh, hd).transpose(0, 2, 1, 3, 4).reshape(bsz * dil, n, nh, hd)

    o, lse = banded_attention(to_cls(q)[:, :, :, None], to_cls(k), to_cls(v), win // dil, math.gcd(n, QUERY_BLOCK))
    o = o[:, :, :, 0].reshape(bsz, dil, n, nh, hd).transpose(0, 2, 1, 3, 4).reshape(bsz, t, nh, hd)
    lse = lse[..., 0].reshape(bsz, dil, n, nh).transpose(0, 2, 1, 3).reshape(bsz, t, nh)
    return o, lse

def mixer_ab(h, lp, past, page_table, is_prompt):
    bsz, t, _ = h.shape
    z, xbc, dt_raw, q, kv, gate = split_cols(h @ lp['w_in'], [SSM_INNER, SSM_CONV_DIM, SSM_HEADS, NSA_HEADS * HEAD_DIM,
                                                          6 * NSA_KV_HEADS * HEAD_DIM, 3 * NSA_HEADS])
    conv_buf = jnp.zeros((bsz, CONV_K - 1, SSM_CONV_DIM), h.dtype) if is_prompt else past['ssm_conv']
    xbc, new_conv = causal_conv(xbc, conv_buf, lp['ssm_conv_w'], lp['ssm_conv_b'])
    xs, bm, cm = split_cols(jax.nn.silu(xbc), [SSM_INNER, SSM_GROUPS * SSM_STATE, SSM_GROUPS * SSM_STATE])
    xs = xs.reshape(bsz, t, SSM_HEADS, SSM_HEAD_DIM)
    bm = bm.reshape(bsz, t, SSM_GROUPS, SSM_STATE)
    cm = cm.reshape(bsz, t, SSM_GROUPS, SSM_STATE)
    dt = jax.nn.softplus(dt_raw.astype(jnp.float32) + lp['ssm_dt_bias'])
    a = -jnp.exp(lp['ssm_a_log'].astype(jnp.float32))
    h0 = jnp.zeros((bsz, SSM_HEADS, SSM_HEAD_DIM, SSM_STATE), jnp.float32) if is_prompt else past['ssm']
    chunk = math.gcd(t, SSM_CHUNK) if is_prompt else t
    y, new_ssm = ssd_scan(xs, dt, a, bm, cm, h0, chunk)
    y = y + lp['ssm_d'].astype(jnp.float32)[:, None] * xs.astype(jnp.float32)
    y_ssm = rmsnorm(y.reshape(bsz, t, SSM_INNER) * jax.nn.silu(z.astype(jnp.float32)), lp['ssm_norm_w']).astype(h.dtype)
    q = q.reshape(bsz, t, NSA_KV_HEADS, NSA_REP, HEAD_DIM)
    kv = kv.reshape(bsz, t, 6, NSA_KV_HEADS, HEAD_DIM)
    rows_new = kv[:, :, 0:4]
    win_new = kv[:, :, 4:6]
    gate = jax.nn.sigmoid(gate.astype(jnp.float32)).reshape(bsz, t, 3, NSA_KV_HEADS, NSA_REP)
    if is_prompt:
        pos = jnp.arange(t)
        rows_all = rows_new
        qblk = math.gcd(t, QUERY_BLOCK)
        o_win, _ = banded_attention(q, win_new[:, :, 0], win_new[:, :, 1], NSA_WINDOW, qblk)
        new_win = win_new[:, t - min(NSA_WINDOW, t):]
    else:
        n_pages = page_table.shape[1]
        past_len = n_pages * PAGE_SIZE
        past_rows = past['nsa_kv'][page_table].reshape(bsz, past_len, 4, NSA_KV_HEADS, HEAD_DIM)
        rows_all = jnp.concatenate([past_rows.astype(rows_new.dtype), rows_new], axis=1)
        pos = past_len + jnp.arange(t)
        qblk = 1
        lw = past['nsa_win'].shape[1]
        win_all = jnp.concatenate([past['nsa_win'].astype(win_new.dtype), win_new], axis=1)
        kpos = past_len - lw + jnp.arange(lw + t)
        diff = pos[:, None] - kpos[None, :]
        o_win, _ = attend_dense(q, win_all[:, :, 0], win_all[:, :, 1], ((diff >= 0) & (diff <= NSA_WINDOW))[None])
        new_win = win_all[:, t:]
    o_cmp, o_sel = nsa_global(q, rows_all[:, :, 0], rows_all[:, :, 1], rows_all[:, :, 2], rows_all[:, :, 3], pos, lp, qblk)
    o_nsa = (gate[:, :, 0, :, :, None] * o_cmp + gate[:, :, 1, :, :, None] * o_sel
             + gate[:, :, 2, :, :, None] * o_win)
    y_nsa = o_nsa.reshape(bsz, t, NSA_HEADS * HEAD_DIM).astype(h.dtype)
    out = jnp.concatenate([y_ssm, y_nsa], axis=-1) @ lp['w_out']
    return out, (new_conv, new_ssm, rows_new, new_win)

def mixer_cd(h, lp, past, is_prompt):
    bsz, t, _ = h.shape
    qkv, z, b_raw, a_raw, dil = split_cols(h @ lp['w_in'], [3 * GDN_WIDTH, GDN_WIDTH, GDN_HEADS, GDN_HEADS, DIL_IN])
    conv_buf = jnp.zeros((bsz, CONV_K - 1, 3 * GDN_WIDTH), h.dtype) if is_prompt else past['gdn_conv']
    qkv, new_conv = causal_conv(qkv, conv_buf, lp['gdn_conv_w'], None)
    qkv = jax.nn.silu(qkv).reshape(bsz, t, 3, GDN_HEADS, GDN_HEAD_DIM)
    q = l2norm(qkv[:, :, 0]) * (GDN_HEAD_DIM ** -0.5)
    k = l2norm(qkv[:, :, 1])
    v = qkv[:, :, 2]
    beta = jax.nn.sigmoid(b_raw.astype(jnp.float32))
    g = -jnp.exp(lp['gdn_a_log'].astype(jnp.float32)) * jax.nn.softplus(a_raw.astype(jnp.float32) + lp['gdn_dt_bias'])
    s0 = jnp.zeros((bsz, GDN_HEADS, GDN_HEAD_DIM, GDN_HEAD_DIM), jnp.float32) if is_prompt else past['gdn']
    chunk = math.gcd(t, GDN_CHUNK) if is_prompt else t
    o, new_gdn = gated_delta(q, k, v, g, beta, s0, chunk)
    o = rmsnorm(o, lp['gdn_norm_w']) * jax.nn.silu(z.astype(jnp.float32)).reshape(bsz, t, GDN_HEADS, GDN_HEAD_DIM)
    y_gdn = o.reshape(bsz, t, GDN_WIDTH).astype(h.dtype)
    dil = dil.reshape(bsz, t, 3, DIL_GROUPS, DIL_HEADS_PER_GROUP, HEAD_DIM)
    outs, lses, bufs = [], [], []
    for gi, (win, dstep) in enumerate(DIL_PATTERNS):
        qg, kg, vg = dil[:, :, 0, gi], dil[:, :, 1, gi], dil[:, :, 2, gi]
        kv_new = jnp.stack([kg, vg], axis=2)
        if is_prompt:
            o_g, lse_g = dilated_prompt(qg, kg, vg, win, dstep)
            bufs.append(kv_new[:, t - min(win, t):])
        else:
            buf = past['dil'][gi]
            lg = buf.shape[1]
            kv_all = jnp.concatenate([buf.astype(kv_new.dtype), kv_new], axis=1)
            n_keys = win // dstep + 1
            idx = lg + jnp.arange(t)[:, None] - dstep * jnp.arange(n_keys)[None, :]
            kv_g = kv_all[:, jnp.maximum(idx, 0)]
            kk = kv_g[:, :, :, 0].transpose(0, 1, 3, 2, 4)
            vv = kv_g[:, :, :, 1].transpose(0, 1, 3, 2, 4)
            o_g, lse_g = attend_gathered(qg[:, :, :, None], kk, vv, (idx >= 0)[None, :, None, :])
            o_g, lse_g = o_g[:, :, :, 0], lse_g[..., 0]
            bufs.append(kv_all[:, t:])
        outs.append(o_g)
        lses.append(lse_g)
    wts = jax.nn.softmax(jnp.stack(lses), axis=0)
    o_dil = jnp.sum(wts[..., None] * jnp.stack(outs).astype(jnp.float32), axis=0)
    y_dil = o_dil.reshape(bsz, t, DIL_HEADS_PER_GROUP * HEAD_DIM).astype(h.dtype)
    out = jnp.concatenate([y_gdn, y_dil], axis=-1) @ lp['w_out']
    return out, (new_conv, new_gdn, bufs[0], bufs[1], bufs[2])

def sq_relu_mlp(h, w1, w2):
    a = jax.nn.relu(h @ w1)
    return (a * a) @ w2

def stack_states(states, i):
    return jnp.stack([s[i] for s in states])

def setup_inputs(seed: int = 0) -> dict:
    key = jax.random.key(seed)
    keys = iter(jax.random.split(key, 64))
    f32 = jnp.float32

    def normal(shape, scale):
        return jax.random.normal(next(keys), shape, f32) * scale

    def gain(shape):
        return 1.0 + normal(shape, 0.02)

    def dt_bias(shape):
        dt = jnp.exp(jax.random.uniform(next(keys), shape, f32, minval=math.log(1e-3), maxval=math.log(1e-1)))
        return dt + jnp.log(-jnp.expm1(-dt))

    def a_log(shape):
        return jnp.log(jax.random.uniform(next(keys), shape, f32, minval=1.0, maxval=16.0))

    n_pages = PAST_LEN // PAGE_SIZE
    n_used = DEC_BATCH * n_pages
    n_phys = n_used + (n_used + 3) // 4
    perm = jax.random.permutation(next(keys), n_phys)
    page_table = perm[:n_used].reshape(DEC_BATCH, n_pages).astype(jnp.int32)
    lw = min(NSA_WINDOW, PAST_LEN)
    dil_kv = [normal((N_CD, DEC_BATCH, min(w, PAST_LEN), 2, DIL_HEADS_PER_GROUP, HEAD_DIM), 1.0) for w, _ in DIL_PATTERNS]
    blk_fan = NSA_BLOCK * HEAD_DIM
    return {
        'x_prompt': normal((BATCH, SEQ, D_MODEL), 1.0),
        'x_sample': normal((DEC_BATCH, DEC_SEQ, D_MODEL), 1.0),
        'cache_ssm_conv': normal((N_AB, DEC_BATCH, CONV_K - 1, SSM_CONV_DIM), 1.0),
        'state_ssm': normal((N_AB, DEC_BATCH, SSM_HEADS, SSM_HEAD_DIM, SSM_STATE), 0.1),
        'cache_nsa_kv': normal((N_AB, n_phys, PAGE_SIZE, 4, NSA_KV_HEADS, HEAD_DIM), 1.0),
        'cache_nsa_win_kv': normal((N_AB, DEC_BATCH, lw, 2, NSA_KV_HEADS, HEAD_DIM), 1.0),
        'cache_gdn_conv': normal((N_CD, DEC_BATCH, CONV_K - 1, 3 * GDN_WIDTH), 1.0),
        'state_gdn': normal((N_CD, DEC_BATCH, GDN_HEADS, GDN_HEAD_DIM, GDN_HEAD_DIM), 0.1),
        'cache_dil0_kv': dil_kv[0],
        'cache_dil1_kv': dil_kv[1],
        'cache_dil2_kv': dil_kv[2],
        'page_table': page_table,
        'norm_mix_pre': gain((DEPTH, D_MODEL)),
        'norm_mix_post': gain((DEPTH, D_MODEL)),
        'norm_mlp_pre': gain((DEPTH, D_MODEL)),
        'norm_mlp_post': gain((DEPTH, D_MODEL)),
        'mlp_w1': normal((DEPTH, D_MODEL, MLP_HIDDEN), D_MODEL ** -0.5),
        'mlp_w2': normal((DEPTH, MLP_HIDDEN, D_MODEL), MLP_HIDDEN ** -0.5),
        'ab_w_in': normal((N_AB, D_MODEL, AB_IN), D_MODEL ** -0.5),
        'ab_w_out': normal((N_AB, AB_MIX, D_MODEL), AB_MIX ** -0.5),
        'ssm_conv_w': normal((N_AB, CONV_K, SSM_CONV_DIM), CONV_K ** -0.5),
        'ssm_conv_b': normal((N_AB, SSM_CONV_DIM), 0.02),
        'ssm_dt_bias': dt_bias((N_AB, SSM_HEADS)),
        'ssm_a_log': a_log((N_AB, SSM_HEADS)),
        'ssm_d': gain((N_AB, SSM_HEADS)),
        'ssm_norm_w': gain((N_AB, SSM_INNER)),
        'nsa_pe_k': normal((N_AB, NSA_BLOCK, HEAD_DIM), 0.1),
        'nsa_pe_v': normal((N_AB, NSA_BLOCK, HEAD_DIM), 0.1),
        'nsa_ck_w1': normal((N_AB, blk_fan, NSA_CMP_HIDDEN), blk_fan ** -0.5),
        'nsa_ck_w2': normal((N_AB, NSA_CMP_HIDDEN, HEAD_DIM), NSA_CMP_HIDDEN ** -0.5),
        'nsa_cv_w1': normal((N_AB, blk_fan, NSA_CMP_HIDDEN), blk_fan ** -0.5),
        'nsa_cv_w2': normal((N_AB, NSA_CMP_HIDDEN, HEAD_DIM), NSA_CMP_HIDDEN ** -0.5),
        'cd_w_in': normal((N_CD, D_MODEL, CD_IN), D_MODEL ** -0.5),
        'cd_w_out': normal((N_CD, CD_MIX, D_MODEL), CD_MIX ** -0.5),
        'gdn_conv_w': normal((N_CD, CONV_K, 3 * GDN_WIDTH), CONV_K ** -0.5),
        'gdn_dt_bias': dt_bias((N_CD, GDN_HEADS)),
        'gdn_a_log': a_log((N_CD, GDN_HEADS)),
        'gdn_norm_w': gain((N_CD, GDN_HEAD_DIM)),
    }

def reference(x_prompt, x_sample, cache_ssm_conv, state_ssm, cache_nsa_kv, cache_nsa_win_kv, cache_gdn_conv, state_gdn,
              cache_dil0_kv, cache_dil1_kv, cache_dil2_kv, page_table, norm_mix_pre, norm_mix_post, norm_mlp_pre,
              norm_mlp_post, mlp_w1, mlp_w2, ab_w_in, ab_w_out, ssm_conv_w, ssm_conv_b, ssm_dt_bias, ssm_a_log, ssm_d,
              ssm_norm_w, nsa_pe_k, nsa_pe_v, nsa_ck_w1, nsa_ck_w2, nsa_cv_w1, nsa_cv_w2, cd_w_in, cd_w_out, gdn_conv_w,
              gdn_dt_bias, gdn_a_log, gdn_norm_w):
    yp, ys = x_prompt, x_sample
    ab_p, ab_s, cd_p, cd_s = [], [], [], []
    for l in range(DEPTH):
        j = l // 2
        hp = rmsnorm(yp, norm_mix_pre[l])
        hs = rmsnorm(ys, norm_mix_pre[l])
        if l % 2 == 0:
            lp = {'w_in': ab_w_in[j], 'w_out': ab_w_out[j], 'ssm_conv_w': ssm_conv_w[j], 'ssm_conv_b': ssm_conv_b[j],
                  'ssm_dt_bias': ssm_dt_bias[j], 'ssm_a_log': ssm_a_log[j], 'ssm_d': ssm_d[j], 'ssm_norm_w': ssm_norm_w[j],
                  'nsa_pe_k': nsa_pe_k[j], 'nsa_pe_v': nsa_pe_v[j], 'nsa_ck_w1': nsa_ck_w1[j], 'nsa_ck_w2': nsa_ck_w2[j],
                  'nsa_cv_w1': nsa_cv_w1[j], 'nsa_cv_w2': nsa_cv_w2[j]}
            past = {'ssm_conv': cache_ssm_conv[j], 'ssm': state_ssm[j], 'nsa_kv': cache_nsa_kv[j], 'nsa_win': cache_nsa_win_kv[j]}
            mp, stp = mixer_ab(hp, lp, None, None, True)
            ms, sts = mixer_ab(hs, lp, past, page_table, False)
            ab_p.append(stp)
            ab_s.append(sts)
        else:
            lp = {'w_in': cd_w_in[j], 'w_out': cd_w_out[j], 'gdn_conv_w': gdn_conv_w[j], 'gdn_dt_bias': gdn_dt_bias[j],
                  'gdn_a_log': gdn_a_log[j], 'gdn_norm_w': gdn_norm_w[j]}
            past = {'gdn_conv': cache_gdn_conv[j], 'gdn': state_gdn[j],
                    'dil': (cache_dil0_kv[j], cache_dil1_kv[j], cache_dil2_kv[j])}
            mp, stp = mixer_cd(hp, lp, None, True)
            ms, sts = mixer_cd(hs, lp, past, False)
            cd_p.append(stp)
            cd_s.append(sts)
        yp = yp + rmsnorm(mp, norm_mix_post[l])
        ys = ys + rmsnorm(ms, norm_mix_post[l])
        yp = yp + rmsnorm(sq_relu_mlp(rmsnorm(yp, norm_mlp_pre[l]), mlp_w1[l], mlp_w2[l]), norm_mlp_post[l])
        ys = ys + rmsnorm(sq_relu_mlp(rmsnorm(ys, norm_mlp_pre[l]), mlp_w1[l], mlp_w2[l]), norm_mlp_post[l])
    return (yp, ys,
            stack_states(ab_p, 0), stack_states(ab_s, 0), stack_states(ab_p, 1), stack_states(ab_s, 1),
            stack_states(ab_p, 2), stack_states(ab_s, 2), stack_states(ab_p, 3), stack_states(ab_s, 3),
            stack_states(cd_p, 0), stack_states(cd_s, 0), stack_states(cd_p, 1), stack_states(cd_s, 1),
            stack_states(cd_p, 2), stack_states(cd_s, 2), stack_states(cd_p, 3), stack_states(cd_s, 3),
            stack_states(cd_p, 4), stack_states(cd_s, 4))


_drawn_inputs = setup_inputs


def setup_inputs(seed=0):
    import zlib

    import numpy as np

    out = dict(_drawn_inputs(seed))
    spreads = {}
    factors = {'norm_mlp_post': 3.035, 'nsa_pe_k': 8.0, 'gdn_norm_w': 6.007}
    for name, (base, spread) in spreads.items():
        noise = np.random.default_rng([zlib.crc32(name.encode()), seed]).standard_normal(out[name].shape)
        drawn = base * np.exp(spread * noise) if base else spread * noise
        out[name] = jnp.asarray(drawn.astype(out[name].dtype))
    for name, factor in factors.items():
        out[name] = (out[name] * factor).astype(out[name].dtype)
    return out
```

```python
from contextlib import ExitStack, contextmanager

import numpy as np

import concourse.bass as bass
from concourse import mybir

F32 = mybir.dt.float32
F32R = mybir.dt.float32r
I32 = mybir.dt.int32
ALU = mybir.AluOpType
ACT = mybir.ActivationFunctionType
AX = mybir.AxisListType

P = 128
D = 1024
KT = D // P
SEQ = 512
NB, NS = 8, 8
TS = NB * NS
NT = SEQ // P
TT = NT + 1
TOK = SEQ + TS
HALF = TOK // 2
TP = TT * P
PAST = 256
PAGE = 128
PAGES = 2
HD = 64
EPS = 1e-6
HID = 4 * D
NEG = -1e30
CONVK = 4

SH = 16
SCONV = 1536
NH = 16
REP = 8
AB_IN = 4416
GH = 8
GW = 1024
DH = 8
DW = DH * HD
CD_IN = 8720
NBLK = SEQ // HD
SBLK = PAST // HD
RING = 3

TILES = [(t, P if t < NT else TS) for t in range(TT)]


class Ctx:
    pass


class Chain:

    def __init__(self, eng, sem):
        self.eng, self.sem, self.n = eng, sem, 0

    def __call__(self, ins):
        ins.then_inc(self.sem, 1)
        self.n += 1
        self.eng.wait_ge(self.sem, self.n)

    def mark(self, ins):
        ins.then_inc(self.sem, 1)
        self.n += 1

    def join(self):
        self.eng.wait_ge(self.sem, self.n)


@contextmanager
def stage(nc, *names):
    at = nc.next_id()
    sems = [nc.alloc_semaphore(f"{name}_{at}") for name in names]
    with nc.Block(no_gpsimd_drain=True) as block:
        yield (block, *sems)
    nc.clear_and_free_semaphores(sems)
    nc.all_engine_barrier()


def bc(ap, axis, n):
    u = ap.unsqueeze(axis)
    shape = list(u.shape)
    shape[axis] = n
    return u.to_broadcast(shape)



def plan_chunks(K):
    plan = []

    def cols(w, c0, n):
        plan.append([(0, P, slice(0, KT), 0, n, w[:, c0:c0 + n].rearrange("(k p) n -> p k n", p=P))])

    def rows(w, k0, kt, c0):
        plan.append([(0, P, slice(0, kt), 0, 512, w[k0 * P:(k0 + kt) * P, c0:c0 + 512]
                      .rearrange("(k p) n -> p k n", p=P))])

    def mlp(layer):
        for up, c in mlp_order():
            if up:
                cols(K.mlp_w1[layer], 512 * c, 512)
            else:
                plan.append([("rows", K.mlp_w2[layer][512 * c:512 * (c + 1), :].rearrange("(k p) n -> p k n", p=P))])

    w = K.ab_w_in[0]
    for c in range(3):
        cols(w, D + 512 * c, 512)
    cols(w, D + SCONV, 16)
    for c in range(2):
        cols(w, 512 * c, 512)
    q0 = D + SCONV + SH
    for c in range(2):
        plan.append([(0, P, slice(0, KT), P * m + HD * g, HD,
                      w[:, q0 + 512 * g + HD * (4 * c + m):q0 + 512 * g + HD * (4 * c + m + 1)]
                      .rearrange("(k p) n -> p k n", p=P)) for m in range(4) for g in range(2)])
    cols(w, q0 + D, 512)
    cols(w, q0 + D + 512, 304)
    for w1 in (K.nsa_ck_w1[0], K.nsa_cv_w1[0]):
        for c in range(2):
            plan.append([(w1[c * 2048:(c + 1) * 2048, :].rearrange("(k p) n -> p k n", p=P),)])
    wo = K.ab_w_out[0]
    for half in range(2):
        rows(wo, 0, 8, 512 * half)
        plan.append([(HD * g, HD * g + HD, slice(0, REP), 0, 512,
                      wo[D + 512 * g:D + 512 * g + 512, 512 * half:512 * half + 512]
                      .rearrange("(m d) n -> d m n", d=HD)) for g in range(2)])
    mlp(0)
    w = K.cd_w_in[0]
    cols(w, 4096, 16)
    for c in range(2):
        cols(w, 3072 + 512 * c, 512)
    for c in range(2):
        for i in range(3):
            cols(w, GW * i + 512 * c, 512)
    for c in range(9):
        cols(w, 4112 + 512 * c, 512)
    wo = K.cd_w_out[0]
    for half in range(2):
        rows(wo, 0, 8, 512 * half)
        rows(wo, 8, 4, 512 * half)
    mlp(1)
    return plan


def fill_ring(K, sp, last, sem=None, uses={}):
    while K.issued <= min(last, len(K.chunks) - 1):
        n = K.issued
        if n - RING in uses:
            sp.wait_ge(*(uses[n - RING] if sem is None else (sem, uses[n - RING])))
        for part in K.chunks[n]:
            if len(part) == 2:
                dst = K.WR[:, n % RING].rearrange("p (k h) n -> p k (h n)", h=2)
            elif len(part) == 1:
                dst = K.WR[:, n % RING].rearrange("p k (e n) -> p (k e) n", e=2)
            else:
                p0, p1, ks, c0, nc_ = part[:5]
                dst = K.WR[p0:p1, n % RING, ks, c0:c0 + nc_]
            sp.dma_start(dst, part[-1]).then_inc(K.w_landed[n % RING], 16)
        K.issued += 1


def chunk_wait(K, pe, n):
    total = sum(len(K.chunks[m]) for m in range(n % RING, n + 1, RING))
    pe.wait_ge(K.w_landed[n % RING], 16 * total)
    return K.WR[:, n % RING]


def inv_rms(act, K, ss, n, summed, count, link):
    act.wait_ge(summed, count)
    act.activation(ss, ss, ACT.Ln, scale=1.0 / n, bias=K.eps[0:ss.shape[0], :]).then_inc(link, 1)
    act.wait_ge(link, 1)
    return act.activation(ss, ss, ACT.Exp, scale=-0.5)



def norm_transpose(nc, K, which, HH=None):
    with ExitStack() as ctx:
        H = ctx.enter_context(nc.sbuf_tensor(f"nrm_h{which}", [P, 2, D], F32))
        SQ = ctx.enter_context(nc.sbuf_tensor(f"nrm_sq{which}", [P, D], F32))
        ss = ctx.enter_context(nc.sbuf_tensor(f"nrm_ss{which}", [P, TT], F32))
        with stage(nc, "sq_done", "rs_done", "h_ready", "t_done", "ht_copied", "rs_link", "hi_done") as (
                block, sq_done, rs_done, h_ready, t_done, ht_copied, rs_link, hi_done):
            @block.scalar
            def _(act):
                for t in range(TT):
                    if t:
                        act.wait_ge(sq_done, t)
                    act.activation(SQ[:], K.X[:, t, :], ACT.Square, accum_out=ss[:, t:t + 1]).then_inc(sq_done, 1)
                inv_rms(act, K, ss[:], D, sq_done, TT, rs_link).then_inc(rs_done, 1)
                if HH is not None:
                    for t in range(TT):
                        act.wait_ge(ht_copied, t + 1)
                        act.copy(HH[:, :, t * P:(t + 1) * P], K.HT[:, :, t * P:(t + 1) * P]).then_inc(hi_done, 1)

            @block.gpsimd
            def _(pool):
                if HH is not None:
                    for t in range(TT):
                        h = K.HT[:, :, t * P:(t + 1) * P]
                        pool.wait_ge(hi_done, t + 1)
                        pool.tensor_tensor(K.HTr[:, :, t * P:(t + 1) * P], h, HH[:, :, t * P:(t + 1) * P].bitcast(F32), ALU.subtract)

            @block.vector
            def _(dve):
                dve.wait_ge(rs_done, 1)
                for t in range(TT + 1):
                    if t < TT:
                        if t >= 2:
                            dve.wait_ge(t_done, t - 1)
                        dve.tensor_scalar(H[:, t % 2, :], K.X[:, t, :], ss[:, t:t + 1], None,
                                          ALU.mult).then_inc(h_ready, 1)
                    if t >= 1:
                        u = t - 1
                        dve.wait_ge(t_done, u + 1)
                        dve.tensor_tensor(K.HT[:, :, u * P:(u + 1) * P],
                                          K.PSF[:, (u % 2) * D:(u % 2) * D + D].rearrange("p (k n) -> p k n", k=KT),
                                          bc(K.normT[:, which, :], 2, P), ALU.mult).then_inc(ht_copied, 1)

            @block.tensor
            def _(pe):
                for t in range(TT):
                    pe.wait_ge(h_ready, t + 1)
                    if t >= 2:
                        pe.wait_ge(ht_copied, t - 1)
                    for k in range(KT):
                        last = pe.transpose(K.PSF[:, (t % 2) * D + k * P:(t % 2) * D + (k + 1) * P],
                                            H[:, t % 2, k * P:(k + 1) * P], K.ident[:])
                    last.then_inc(t_done, 1)



def proj_matmuls(K, pe, W, mode, at, pair, n=512):
    base = pair * 1024
    if mode == "T":
        for b in range(2):
            for k in range(KT):
                w = W[:, k, at * P:(at + 1) * P]
                last = pe.matmul(K.PS[:, 2 * pair + b, 0:HALF], w, K.HT[:, k, b * HALF:(b + 1) * HALF],
                                 start=(k == 0), stop=(k == KT - 1))
    else:
        rows = TILES[at][1]
        for k in range(KT):
            last = pe.matmul(K.PSF[0:rows, base:base + n], K.HT[:, k, at * P:at * P + rows], W[:, k, 0:n],
                             start=(k == 0), stop=(k == KT - 1))
    return last


def project(nc, K, name, units, post=None):
    done_by = {"act": [0], "dve": [0]}
    for u in units:
        for e in done_by:
            done_by[e].append(done_by[e][-1] + (u[4] == e))
    with stage(nc, f"{name}_mm", f"{name}_act", f"{name}_dve") as (block, mm_done, act_done, dve_done):
        sem = {"act": act_done, "dve": dve_done}

        @block.sync
        def _(sp):
            fill_ring(K, sp, units[-1][0] + RING, mm_done, {u[0]: i + 1 for i, u in enumerate(units)})

        @block.tensor
        def _(pe):
            for i, (chunk, mode, at, n, eng, _) in enumerate(units):
                if i == 0 or units[i - 1][0] != chunk:
                    W = chunk_wait(K, pe, chunk)
                if i >= 4:
                    e = units[i - 4][4]
                    pe.wait_ge(sem[e], done_by[e][i - 3])
                last = proj_matmuls(K, pe, W, mode, at, i % 4, n)
                last.then_inc(mm_done, 1)

        def evacuate(eng, name_):
            for i, (chunk, mode, at, n, e, evac) in enumerate(units):
                if e == name_:
                    eng.wait_ge(mm_done, i + 1)
                    evac(eng, i % 4, at).then_inc(sem[e], 1)

        @block.scalar
        def _(act):
            evacuate(act, "act")

        @block.vector
        def _(dve):
            evacuate(dve, "dve")
            if post:
                for i in range(len(units)):
                    dve.wait_ge(act_done, i + 1)
                    post(dve, i)


def both_halves(K, pair):
    return K.PS[:, 2 * pair:2 * pair + 2, 0:HALF]


def in_halves(ap):
    return ap.rearrange("p (b n) -> p b n", b=2)


def copy_on(eng, out, in_):
    return eng.copy(out, in_) if eng.engine == mybir.EngineType.Activation else eng.tensor_copy(out, in_)



def initialise(nc, K):
    with ExitStack() as ctx:
        def tmp(name, shape, dt=I32):
            return ctx.enter_context(nc.sbuf_tensor(name, shape, dt))

        diff = tmp("i_diff", [P, P])
        xr = tmp("i_xor", [P, P])
        fi = tmp("i_free", [P, P])
        pi = tmp("i_part", [P, P])
        t1 = tmp("i_t1", [P, P])
        same8 = tmp("i_same8", [P, P])
        cb = tmp("i_cb", [P, NT, NBLK])
        selc = tmp("i_selc", [P, TS])
        step = tmp("i_step", [P, 1])
        own = tmp("i_own", [P, 15, NS])
        own2 = tmp("i_own2", [P, 15, NS])
        own3 = tmp("i_own3", [P, 15, NS])
        table = tmp("i_table", [1, NB * PAGES])
        with stage(nc, "iota_done", "dve_link", "pool_set", "table_in", "x_zero") as (
                block, iota_done, dve_link, pool_set, table_in, x_zero):
            @block.sync
            def _(sp):
                sp.dma_start(table[:], K.page_table.rearrange("b n -> (b n)").unsqueeze(0)).then_inc(table_in, 16)
                sp.dma_start(K.X[:, 0:NT, :], K.x_prompt[0].rearrange("(t p) d -> p t d", p=P)).then_inc(K.x_in, 16)
                sp.dma_start(K.X[0:TS, NT, :], K.x_sample.rearrange("b s d -> (b s) d")).then_inc(K.x_in, 16)
                fill_ring(K, sp, RING - 1)
                sp.wait_ge(table_in, 16)
                for b in range(NB):
                    for n in range(PAGES):
                        page = sp.value_load(table[0:1, b * PAGES + n:b * PAGES + n + 1], min_val=0,
                                             max_val=K.n_phys - 1)
                        sp.dma_start(K.past[b, n * PAGE:(n + 1) * PAGE, :],
                                     K.nsa_kv[0].rearrange("n r k g d -> n r (k g d)")[bass.ds(page, 1), :, :]
                                     .rearrange("n r c -> (n r) c")).then_inc(K.past_in, 16)
                sp.wait_ge(K.x_in, 32)

            @block.scalar
            def _(act):
                for i, w in enumerate((K.norm_mix_pre[0], K.norm_mlp_pre[0], K.norm_mix_pre[1], K.norm_mlp_pre[1])):
                    act.dma_start(K.normT[:, i, :], w.rearrange("(k p) -> p k", p=P),
                                  allow_slow_non_contiguous=True).then_inc(K.small_in, 16)
                act.wait_ge(K.small_in, 64)

            @block.gpsimd
            def _(pool):
                pool.memset(K.X[64:P, NT, :], 0.0).then_inc(x_zero, 1)
                pool.wait_ge(x_zero, 1)
                pool.memset(K.eps[:], EPS).then_inc(x_zero, 1)
                pool.memset(K.ones[:], 1.0).then_inc(x_zero, 1)
                pool.iota(diff[:], [[1, P]], base=1024, channel_multiplier=-1).then_inc(iota_done, 1)
                pool.iota(fi[:], [[1, P]], base=0, channel_multiplier=0).then_inc(iota_done, 1)
                pool.iota(pi[:], [[0, P]], base=0, channel_multiplier=1).then_inc(iota_done, 1)
                pool.iota(cb[:], [[P, NT], [-HD, NBLK]], base=1 - HD, channel_multiplier=1).then_inc(iota_done, 1)
                pool.iota(selc[:], [[1, TS]], base=0, channel_multiplier=0).then_inc(iota_done, 1)
                pool.iota(step[:], [[0, 1]], base=0, channel_multiplier=1).then_inc(iota_done, 1)
                pool.iota(own[:], [[NS, 15], [1, NS]], base=-7 * NS, channel_multiplier=0).then_inc(iota_done, 1)

            @block.vector
            def _(dve):
                do = Chain(dve, dve_link)
                dve.wait_ge(iota_done, 7)

                def ts(out, in_, a, b, op0, op1=None):
                    if op1 is None:
                        do(dve.tensor_scalar(out, in_, a, None, op0))
                    else:
                        do(dve.tensor_scalar(out, in_, a, b, op0, op1))

                def tt(out, a, b, op):
                    do(dve.tensor_tensor(out, a, b, op))

                tt(xr[:], fi[:], pi[:], ALU.bitwise_xor)
                ts(K.ident[:], diff[:], 1024, None, ALU.is_equal)
                ts(same8[:], xr[:], 8, None, ALU.is_lt)
                ts(t1[:], diff[:], 1024, None, ALU.is_ge)
                for t in range(NT):
                    ts(K.U5[:, t, :], diff[:], 1024, None, ALU.is_ge)
                tt(K.U5[:, NT, :], t1[:], same8[:], ALU.mult)
                ts(K.NM5, K.U5, -1.0, -NEG, ALU.add, ALU.mult)
                ts(K.B8[:], same8[:], 1, None, ALU.mult)
                ts(K.CV[:], cb[:], 0, None, ALU.is_ge)
                ts(K.CN[:], K.CV[:], -1.0, -NEG, ALU.add, ALU.mult)
                ts(t1[:], fi[:], 7, None, ALU.bitwise_and)
                tt(K.R8[:], t1[0:8, :], pi[0:8, :], ALU.is_equal)
                ts(t1[:, 0:NH], pi[:, 0:NH], 3, None, ALU.logical_shift_right)
                tt(K.SELH[:], t1[:, 0:NH], fi[:, 0:NH], ALU.is_equal)
                ts(selc[:], selc[:], 3, None, ALU.logical_shift_right)
                for b in range(NB):
                    ts(K.SELC[:, b, :], selc[:], b, None, ALU.is_equal)
                ts(t1[:, 0:1], step[:], 3, None, ALU.logical_shift_right)
                for b in range(NB):
                    ts(K.SELT[:, b:b + 1], t1[:, 0:1], b, None, ALU.is_equal)
                ts(step[:], step[:], 3, None, ALU.logical_shift_right)
                ts(step[:], step[:], 7, None, ALU.bitwise_and)
                so = bc(step[:, 0:1].to_broadcast([P, NS]), 1, 15)
                tt(own2[:], so, own[:], ALU.subtract)
                ts(own3[:], own[:], 0, None, ALU.is_ge)
                do(dve.tensor_tensor(own3[:, 8:, :], own3[:, 8:, :], own3[:, 8:, :], ALU.subtract))
                for g, dil in ((0, 1), (1, 4), (2, 16)):
                    ts(own[:], own2[:], 256, None, ALU.add)
                    ts(own[:], own[:], dil - 1, None, ALU.bitwise_and)
                    ts(own[:], own[:], 0, None, ALU.is_equal)
                    tt(own[:], own[:], own3[:], ALU.mult)
                    ts(K.MO[:, g], own2[:], 0, None, ALU.is_ge)
                    tt(K.MO[:, g], K.MO[:, g], own[:], ALU.mult)
                    ts(K.MO[:, g], K.MO[:, g], -1.0, -NEG, ALU.add, ALU.mult)
                ts(K.CM[:], diff[:], 1024, NEG, ALU.is_gt, ALU.mult)
                dve.wait_ge(x_zero, 3)


def gdn_masks(nc, K):
    with ExitStack() as ctx:
        def tmp(name):
            return ctx.enter_context(nc.sbuf_tensor(name, [P, P], I32))

        diff, xr, fi, pi, t1, t2, lo = (tmp(f"l_{n}") for n in ("diff", "xr", "fi", "pi", "t1", "t2", "lo"))
        with stage(nc, "iota_done", "dve_link") as (block, iota_done, dve_link):
            @block.gpsimd
            def _(pool):
                pool.iota(diff[:], [[1, P]], base=1024, channel_multiplier=-1).then_inc(iota_done, 1)
                pool.iota(fi[:], [[1, P]], base=0, channel_multiplier=0).then_inc(iota_done, 1)
                pool.iota(pi[:], [[0, P]], base=0, channel_multiplier=1).then_inc(iota_done, 1)

            @block.vector
            def _(dve):
                do = Chain(dve, dve_link)
                dve.wait_ge(iota_done, 3)
                do(dve.tensor_tensor(xr[:], fi[:], pi[:], ALU.bitwise_xor))
                do(dve.tensor_scalar(lo[:], diff[:], 1024, None, ALU.is_gt))
                for k in range(7):
                    do(dve.tensor_scalar(t1[:], xr[:], 1 << k, None, ALU.is_ge))
                    do(dve.tensor_scalar(t2[:], xr[:], 2 << k, None, ALU.is_lt))
                    do(dve.tensor_tensor(t1[:], t1[:], t2[:], ALU.mult))
                    do(dve.tensor_tensor(K.LV[:, k, :], t1[:], lo[:], ALU.mult))


def dilated_masks(nc, K):
    with ExitStack() as ctx:
        def tmp(name, shape, dt=I32):
            return ctx.enter_context(nc.sbuf_tensor(name, shape, dt))

        diff = tmp("j_diff", [P, P])
        t1 = tmp("j_t1", [P, P])
        t2 = tmp("j_t2", [P, P])
        step = tmp("j_step", [P, 1])
        key = tmp("j_key", [P, PAST])
        kd = tmp("j_kd", [P, PAST])
        kd2 = tmp("j_kd2", [P, PAST])
        hm = tmp("j_hm", [P, DH // 2, DH])
        half = tmp("j_half", [P, 1])
        with stage(nc, "iota_done", "dve_link") as (block, iota_done, dve_link):
            @block.gpsimd
            def _(pool):
                pool.iota(diff[:], [[1, P]], base=1024, channel_multiplier=-1).then_inc(iota_done, 1)
                pool.iota(step[:], [[0, 1]], base=0, channel_multiplier=1).then_inc(iota_done, 1)
                pool.iota(key[:], [[-1, PAST]], base=PAST, channel_multiplier=0).then_inc(iota_done, 1)
                pool.iota(hm[:], [[-2, DH // 2], [1, DH]], base=0, channel_multiplier=0).then_inc(iota_done, 1)
                pool.iota(half[:], [[0, 1]], base=0, channel_multiplier=1).then_inc(iota_done, 1)

            @block.vector
            def _(dve):
                do = Chain(dve, dve_link)
                dve.wait_ge(iota_done, 5)

                def ts(out, in_, a, b, op0, op1=None):
                    if op1 is None:
                        do(dve.tensor_scalar(out, in_, a, None, op0))
                    else:
                        do(dve.tensor_scalar(out, in_, a, b, op0, op1))

                def tt(out, a, b, op):
                    do(dve.tensor_tensor(out, a, b, op))

                ts(t2[:], diff[:], 1024, None, ALU.is_le)
                ts(K.MJ[:, 0:P], diff[:], 1024, NEG, ALU.is_lt, ALU.mult)
                ts(K.MJ[:, P:2 * P], diff[:], 1024, NEG, ALU.is_gt, ALU.mult)
                for g, dil in ((1, 4), (2, 16)):
                    ts(t1[:], diff[:], dil - 1, None, ALU.bitwise_and)
                    base = 256 + 512 * (g - 1)
                    for t in range(NT - 1):
                        ts(K.MJ[:, base + t * P:base + (t + 1) * P], t1[:], 0, NEG, ALU.is_gt, ALU.mult)
                    ts(t1[:], t1[:], 0, None, ALU.is_equal)
                    tt(t1[:], t1[:], t2[:], ALU.mult)
                    ts(K.MJ[:, base + 384:base + 512], t1[:], 0, NEG, ALU.is_equal, ALU.mult)
                ts(half[:], half[:], 6, None, ALU.logical_shift_right)
                tt(K.HM[:].rearrange("p a h -> p (a h)"), hm[:].rearrange("p a h -> p (a h)"),
                   half[:, 0:1].to_broadcast([P, DH // 2 * DH]), ALU.is_equal)
                ts(step[:], step[:], 3, None, ALU.logical_shift_right)
                ts(step[:], step[:], 7, None, ALU.bitwise_and)
                st = step[:, 0:1].to_broadcast([P, PAST])
                tt(kd[:], key[:], st, ALU.add)
                ts(K.MS[:, 0:P], kd[:, P:PAST], P, NEG, ALU.is_gt, ALU.mult)
                for g, dil in ((1, 4), (2, 16)):
                    ts(kd2[:], kd[:], dil - 1, None, ALU.bitwise_and)
                    ts(K.MS[:, P + PAST * (g - 1):P + PAST * g], kd2[:], 0, NEG, ALU.is_gt, ALU.mult)



def conv_inputs(nc, K, CC, n_ch, hist_dram, w_dram, b_dram, hist, wT, cols, work):
    nw = CONVK + (b_dram is not None)
    rows, taps = work[:, 0:CC], work[:, CC:2 * CC]
    nh = NB * (CONVK - 1)
    with stage(nc, "rows_in", "turned", "copied") as (block, rows_in, turned, copied):
        @block.scalar
        def _(act):
            for to, at, n in cols:
                act.dma_start(rows[0:nh, to:to + n], hist_dram[:, :, at:at + n].rearrange("b s c -> (b s) c")).then_inc(rows_in, 16)
                act.dma_start(taps[0:CONVK, to:to + n], w_dram[:, at:at + n]).then_inc(rows_in, 16)
            if b_dram is not None:
                act.dma_start(taps[CONVK:nw, :], b_dram.unsqueeze(0)).then_inc(rows_in, 16)

        @block.tensor
        def _(pe):
            pe.wait_ge(rows_in, 16 * (2 * len(cols) + nw - CONVK))
            for c in range(n_ch):
                if c >= 4:
                    pe.wait_ge(copied, 2 * (c - 3))
                pe.transpose(K.PS[:, c % 4, 0:nh], rows[0:nh, c * P:(c + 1) * P], K.ident[0:nh, 0:nh])
                pe.transpose(K.PS[:, c % 4, 64:64 + nw], taps[0:nw, c * P:(c + 1) * P],
                             K.ident[0:nw, 0:nw]).then_inc(turned, 1)

        @block.vector
        def _(dve):
            for c in range(n_ch):
                dve.wait_ge(turned, c + 1)
                dve.tensor_copy(hist[:, c], K.PS[:, c % 4, 0:nh].rearrange("p (b s) -> p b s", b=NB)).then_inc(copied, 1)
                dve.tensor_copy(wT[:, c, 0:nw], K.PS[:, c % 4, 64:64 + nw]).then_inc(copied, 1)


def project_conv(nc, K, name, first, n_ch, hist, wT, bias, SX, keep, work):
    PW, SW = CONVK - 1 + SEQ, CONVK - 1 + NS
    XW = 2 * (PW + NB * SW)
    XC = work[:, 0:XW].rearrange("p (s n) -> p s n", s=2)
    CO = work[:, XW:XW + 2 * TOK].rearrange("p (s n) -> p s n", s=2)
    with stage(nc, f"{name}_mm", f"{name}_raw", f"{name}_kept", f"{name}_tap", f"{name}_conv",
               f"{name}_silu", f"{name}_zero") as (block, mm_done, raw_ready, kept, tap, conv_done, silu_done, zeroed):
        @block.sync
        def _(sp):
            fill_ring(K, sp, first + n_ch // 4 - 1 + RING, mm_done,
                      {first + c: 4 * c + 4 for c in range(n_ch // 4)})

        @block.gpsimd
        def _(pool):
            for j in range(2):
                pool.memset(XC[:, j, 0:CONVK - 1], 0.0).then_inc(zeroed, 1)
            pool.memset(SX[:, :, TOK:TP], 0.0).then_inc(zeroed, 1)

        @block.tensor
        def _(pe):
            for u in range(n_ch):
                if u % 4 == 0:
                    W = chunk_wait(K, pe, first + u // 4)
                if u >= 4:
                    pe.wait_ge(raw_ready, 4 * (u - 3))
                proj_matmuls(K, pe, W, "T", u % 4, u % 4).then_inc(mm_done, 1)

        def silu(act, u):
            act.wait_ge(conv_done, u + 1)
            act.activation(SX[:, u, 0:TOK], CO[:, u % 2, :], ACT.Silu).then_inc(silu_done, 1)

        @block.scalar
        def _(act):
            for u in range(n_ch):
                act.wait_ge(mm_done, u + 1)
                if u >= 2:
                    act.wait_ge(conv_done, u - 1)
                    act.wait_ge(kept, u - 1)
                s = XC[:, u % 2, PW:].rearrange("p (b s) -> p b s", b=NB)
                b = 2 * (u % 4)
                act.copy(XC[:, u % 2, CONVK - 1:CONVK - 1 + HALF], K.PS[:, b, 0:HALF]).then_inc(raw_ready, 1)
                act.copy(XC[:, u % 2, CONVK - 1 + HALF:PW], K.PS[:, b + 1, 0:SEQ - HALF]).then_inc(raw_ready, 1)
                act.copy(s[:, :, CONVK - 1:], K.PS[:, b + 1, SEQ - HALF:HALF].rearrange("p (b s) -> p b s", b=NB)).then_inc(raw_ready, 1)
                act.copy(s[:, :, 0:CONVK - 1], hist[:, u]).then_inc(raw_ready, 1)
                if u >= 1:
                    silu(act, u - 1)
            silu(act, n_ch - 1)

        @block.vector
        def _(dve):
            dve.wait_ge(zeroed, 3)
            n = 0
            for u in range(n_ch):
                dve.wait_ge(raw_ready, 4 * (u + 1))
                s = XC[:, u % 2, PW:].rearrange("p (b s) -> p b s", b=NB)
                dve.tensor_copy(keep[:, u, 0:3], XC[:, u % 2, PW - 3:PW])
                dve.tensor_copy(keep[:, u, 3:27].rearrange("p (b s) -> p b s", b=NB), s[:, :, NS:]).then_inc(kept, 1)
                if u >= 2:
                    dve.wait_ge(silu_done, u - 1)
                op = CO[:, u % 2, 0:SEQ]
                os_ = CO[:, u % 2, SEQ:].rearrange("p (b s) -> p b s", b=NB)
                for i in range(CONVK):
                    w = wT[:, u, i:i + 1]
                    xp, xs = XC[:, u % 2, i:i + SEQ], s[:, :, i:i + NS]
                    if i == 0:
                        if bias:
                            dve.tensor_scalar(op, xp, w, wT[:, u, CONVK:CONVK + 1], ALU.mult, ALU.add).then_inc(tap, 1)
                            dve.tensor_scalar(os_, xs, w, wT[:, u, CONVK:CONVK + 1], ALU.mult, ALU.add).then_inc(tap, 1)
                        else:
                            dve.tensor_scalar(op, xp, w, None, ALU.mult).then_inc(tap, 1)
                            dve.tensor_scalar(os_, xs, w, None, ALU.mult).then_inc(tap, 1)
                        n += 2
                    else:
                        dve.wait_ge(tap, n - 1)
                        a = dve.scalar_tensor_tensor(op, xp, w, op, ALU.mult, ALU.add)
                        a.then_inc(tap, 1)
                        dve.wait_ge(tap, n)
                        b = dve.scalar_tensor_tensor(os_, xs, w, os_, ALU.mult, ALU.add)
                        b.then_inc(conv_done if i == CONVK - 1 else tap, 1)
                        n += 2 - (i == CONVK - 1)


def write_conv_state(nc, K, n_ch, keep, out_p, out_s, cols):
    rows = K.conv_rows
    with stage(nc, "turned", "copied") as (block, turned, copied):
        @block.tensor
        def _(pe):
            for c in range(n_ch):
                if c >= 8:
                    pe.wait_ge(copied, c - 7)
                pe.transpose(K.PS[0:27, c % 8, 0:P], keep[:, c, :], K.ident[:]).then_inc(turned, 1)

        @block.vector
        def _(dve):
            for c in range(n_ch):
                dve.wait_ge(turned, c + 1)
                dve.tensor_copy(rows[0:27, c * P:(c + 1) * P], K.PS[0:27, c % 8, 0:P]).then_inc(copied, 1)

        @block.sync
        def _(sp):
            sp.wait_ge(copied, n_ch)
            for to, at, n in cols:
                sp.dma_start(out_p[0, :, at:at + n], rows[0:3, to:to + n]).then_inc(K.state_out, 16)
                sp.dma_start(out_s[:, :, at:at + n].rearrange("b s c -> (b s) c"), rows[3:27, to:to + n]).then_inc(K.state_out, 16)
            K.n_state_out += 2 * len(cols)
            sp.wait_ge(K.state_out, 16 * K.n_state_out)


def log1p_series(do, dve, x, y, s, q):
    do(dve.tensor_scalar(s, y, 2.0, None, ALU.add))
    do(dve.reciprocal(s, s))
    do(dve.tensor_tensor(s, s, y, ALU.mult))
    do(dve.tensor_tensor(y, s, s, ALU.mult))
    do(dve.memset(q, 2.0 / 17))
    for k in range(7, -1, -1):
        do(dve.tensor_tensor(q, q, y, ALU.mult))
        do(dve.tensor_scalar(q, q, 2.0 / (2 * k + 1), None, ALU.add))
    do(dve.tensor_tensor(q, q, s, ALU.mult))
    do(dve.scalar_tensor_tensor(x, x, 0.0, q, ALU.max, ALU.add))



def ssm(nc, K, chunk):
    NCH = SCONV // P
    with ExitStack() as ctx:
        def sb(name, shape):
            return ctx.enter_context(nc.sbuf_tensor(name, shape, F32))

        SX = sb("s_SX", [P, NCH, TP])
        YTF = K.YT[:].rearrange("p k n -> p (k n)")
        Y = YTF[:, KT * TP:].rearrange("p (t d) -> p t d", t=TT)
        dt = sb("s_dt", [P, TT, SH])
        la = sb("s_la", [P, TT, SH])
        dlast = sb("s_dlast", [P, TT, SH])
        acs = sb("s_acs", [P, TT, SH])
        eacs = sb("s_eacs", [P, TT, SH])
        sm = [sb(f"s_sm{i}", [P, TT * SH]) for i in range(3)]
        rowp = sb("s_rowp", [P, 3, SH])
        with ExitStack() as c2:
            hist = c2.enter_context(nc.sbuf_tensor("s_hist", [P, NCH, NB, CONVK - 1], F32))
            wT = c2.enter_context(nc.sbuf_tensor("s_wT", [P, NCH, CONVK + 1], F32))
            keep = c2.enter_context(nc.sbuf_tensor("s_keep", [P, NCH, 27], F32))
            K.conv_rows = YTF[:, KT * TP:]
            cols = [(0, 0, SCONV)]
            conv_inputs(nc, K, SCONV, NCH, K.ssm_conv[0], K.ssm_conv_w[0], K.ssm_conv_b[0], hist, wT, cols, K.conv_rows)
            project_conv(nc, K, "sconv", chunk, NCH, hist, wT, True, SX, keep, K.conv_rows)
            write_conv_state(nc, K, NCH, keep, K.o_ssm_conv_p[0], K.o_ssm_conv_s[0], cols)

        with stage(nc, "rows_in", "dt_mm", "dve_link", "exp_in", "exp_out", "cum_mm", "cum_out") as (
                block, rows_in, dt_mm, dve_link, exp_in, exp_out, cum_mm, cum_out):
            U = TT * SH
            dtf, laf, lf, af, ef = (x[:].rearrange("p t h -> p (t h)") for x in (dt, la, dlast, acs, eacs))

            @block.sync
            def _(sp):
                fill_ring(K, sp, chunk + 3 + RING, dt_mm, {chunk + 3: 1})

            @block.scalar
            def _(act):
                for i, r in enumerate((K.ssm_a_log, K.ssm_dt_bias, K.ssm_d)):
                    act.dma_start(rowp[:, i, :], r[0].partition_broadcast(P)).then_inc(rows_in, 16)
                act.wait_ge(rows_in, 48)
                act.activation(rowp[:, 0, :], rowp[:, 0, :], ACT.Exp).then_inc(exp_out, 1)
                act.wait_ge(exp_in, 1)
                act.activation(sm[0][:], sm[0][:], ACT.Exp, scale=-1.0).then_inc(exp_out, 1)
                act.wait_ge(cum_out, 1)
                act.activation(lf, lf, ACT.Exp).then_inc(exp_out, 1)
                act.activation(ef, af, ACT.Exp).then_inc(exp_out, 1)
                act.wait_ge(exp_out, 4)

            @block.tensor
            def _(pe):
                W = chunk_wait(K, pe, chunk + 3)
                for t in range(TT):
                    for k in range(KT):
                        last = pe.matmul(K.PS[:, 0, t * SH:(t + 1) * SH], K.HT[:, k, t * P:(t + 1) * P],
                                         W[:, k, 0:SH], start=(k == 0), stop=(k == KT - 1))
                last.then_inc(dt_mm, 1)
                pe.wait_ge(cum_mm, 1)
                for t in range(TT):
                    pe.matmul(K.PS[:, 1, t * SH:(t + 1) * SH], K.U5[:, t, :], la[:, t, :], start=True, stop=True)
                    last = pe.matmul(K.PS[:, 2, t * SH:(t + 1) * SH], K.ones[:] if t < NT else K.B8[:], la[:, t, :],
                                     start=True, stop=True)
                last.then_inc(dt_mm, 1)

            @block.vector
            def _(dve):
                do = Chain(dve, dve_link)
                dve.wait_ge(rows_in, 48)
                dve.wait_ge(exp_out, 1)
                dve.wait_ge(dt_mm, 1)
                do(dve.tensor_tensor(dt[:], K.PS[:, 0, 0:U].rearrange("p (t h) -> p t h", h=SH),
                                     bc(rowp[:, 1, :], 1, TT), ALU.add))

                dve.scalar_tensor_tensor(sm[0][:], dtf, -1.0, dtf, ALU.mult, ALU.max).then_inc(exp_in, 1)
                dve.wait_ge(exp_out, 2)
                log1p_series(do, dve, dtf, sm[0][:], sm[1][:], sm[2][:])
                do(dve.tensor_tensor(la[:], dt[:], bc(rowp[:, 0, :], 1, TT), ALU.mult))
                dve.tensor_scalar(laf, laf, -1.0, None, ALU.mult).then_inc(cum_mm, 1)
                dve.wait_ge(dt_mm, 2)
                do(dve.tensor_copy(af, K.PS[:, 1, 0:U]))
                dve.tensor_tensor(lf, K.PS[:, 2, 0:U], af, ALU.subtract).then_inc(cum_out, 1)
        ssd_tiles(nc, K, SX, Y, dt, la, dlast, acs, eacs, rowp)
        ssm_gate(nc, K, Y, chunk + 4)
        ssm_norm(nc, K, Y)


def ssd_tiles(nc, K, SX, Y, dt, la, dlast, acs, eacs, rowp):
    with ExitStack() as ctx:
        def sb(name, shape):
            return ctx.enter_context(nc.sbuf_tensor(name, shape, F32))

        XX = sb("d_xx", [P, 2, D])
        xtok = XX[:, 0, :]
        xd = XX[:, 1, :]
        xdw = sb("d_xdw", [P, D])
        YD = sb("d_YD", [P, D])
        Btok = sb("d_Btok", [P, 256])
        H = sb("d_H", [P, D])
        with ExitStack() as c2:
            low = K.YT[:, 0:KT, :].rearrange("p k n -> p (k n)")
            UL = low[:, 0:1024].rearrange("p (s h n) -> p s h n", s=2, h=4)
            DD = low[:, 1024:2048].rearrange("p (s h n) -> p s h n", s=2, h=4)
            M = low[:, 2048:4096].rearrange("p (h n) -> p h n", h=SH)
            CB = c2.enter_context(nc.sbuf_tensor("d_CB", [P, 2, P], F32))
            rl = c2.enter_context(nc.sbuf_tensor("d_rl", [P, SH], F32))
            ehl = c2.enter_context(nc.sbuf_tensor("d_ehl", [P, SH], F32))
            with stage(nc, "tr_done", "x_copied", "ul_ready", "yd_ready", "dve_tok", "r_done", "r_read", "d_ready",
                       "m_exp", "m_ready", "ehl_ready", "diag_done", "off_done", "s_done", "y_done", "h_ready",
                       "dve_link") as (block, tr_done, x_copied, ul_ready, yd_ready, dve_tok, r_done, r_read,
                                       d_ready, m_exp, m_ready, ehl_ready, diag_done, off_done, s_done, y_done,
                                       h_ready, dve_link):
                def heads(ap):
                    return ap.rearrange("p (h q) -> p h q", h=SH)

                @block.tensor
                def _(pe):
                    for t in range(TT):
                        ts_ = slice(t * P, (t + 1) * P)
                        if t:
                            pe.wait_ge(y_done, t)
                            pe.wait_ge(dve_tok, t)
                        for c in range(8):
                            pe.transpose(K.PSF[:, c * P:(c + 1) * P], SX[:, c, ts_], K.ident[:])
                        for g in range(2):
                            pe.transpose(K.PS[:, 2, g * P:(g + 1) * P], SX[:, 8 + g, ts_], K.ident[:])
                        for g in range(2):
                            last = pe.matmul(K.PS[:, 2, 256 + g * P:256 + (g + 1) * P], SX[:, 8 + g, ts_],
                                             SX[:, 10 + g, ts_], start=True, stop=True)
                        last.then_inc(tr_done, 1)
                        for hq in range(4):
                            n = 4 * t + hq
                            pe.wait_ge(ul_ready, n + 1)
                            if n >= 2:
                                pe.wait_ge(r_read, n - 1)
                            if 1 <= t and hq < 2:
                                pe.wait_ge(h_ready, min(t, NT))
                            pe.matmul(K.PS[:, 3 + hq % 2, :], K.ones[:], UL[:, hq % 2].rearrange("p h n -> p (h n)"),
                                      start=True, stop=True).then_inc(r_done, 1)
                        pe.wait_ge(m_ready, 4 * t + 4)
                        for h in range(SH):
                            last = pe.matmul(K.PSF[:, 2560 + h * HD:2560 + (h + 1) * HD], M[:, h, :],
                                             xd[:, h * HD:(h + 1) * HD], start=True, stop=True)
                        last.then_inc(diag_done, 1)
                        if 1 <= t < NT:
                            pe.wait_ge(h_ready, t)
                            pe.wait_ge(x_copied, t + 1)
                            for g in range(2):
                                last = pe.matmul(K.PS[:, g, :], SX[:, 10 + g, ts_], H[:, g * 512:(g + 1) * 512],
                                                 start=True, stop=True)
                            last.then_inc(off_done, 1)
                        if t < NT:
                            pe.wait_ge(r_read, 4 * t + 4)
                            for g in range(2):
                                last = pe.matmul(K.PS[:, 3 + g, :], Btok[:, g * P:(g + 1) * P],
                                                 xdw[:, g * 512:(g + 1) * 512], start=True, stop=True)
                            last.then_inc(s_done, 1)

                @block.gpsimd
                def _(pool):
                    for t in range(TT):
                        for hq in range(4):
                            n = 4 * t + hq
                            if n >= 2:
                                pool.wait_ge(r_done, n - 1)
                            pool.tensor_tensor(UL[:, hq % 2], bc(K.U5[:, t, :], 1, 4),
                                               bc(la[:, t, 4 * hq:4 * hq + 4], 2, P), ALU.mult).then_inc(ul_ready, 1)
                        pool.wait_ge(x_copied, t + 1)
                        if t:
                            pool.wait_ge(y_done, t)
                        pool.tensor_tensor(heads(YD[:]), heads(xtok), bc(rowp[:, 2, :], 2, HD),
                                           ALU.mult).then_inc(yd_ready, 1)

                @block.scalar
                def _(act):
                    for t in range(TT):
                        act.wait_ge(tr_done, t + 1)
                        if t:
                            act.wait_ge(yd_ready, t)
                            act.wait_ge(dve_tok, t)
                            act.wait_ge(diag_done, t)
                        act.copy(xtok, K.PSF[:, 0:D]).then_inc(x_copied, 1)
                        for hq in range(4):
                            n = 4 * t + hq
                            act.wait_ge(d_ready, n + 1)
                            act.activation(M[:, 4 * hq:4 * hq + 4, :], DD[:, hq % 2], ACT.Exp).then_inc(m_exp, 1)
                        if t < NT:
                            if t:
                                act.wait_ge(h_ready, t)
                            act.activation(ehl[:], rl[:], ACT.Exp).then_inc(ehl_ready, 1)

                @block.vector
                def _(dve):
                    do = Chain(dve, dve_link)
                    for t in range(TT):
                        dve.wait_ge(tr_done, t + 1)
                        if t:
                            dve.wait_ge(diag_done, t)
                            dve.wait_ge(s_done, min(t, NT))
                        dve.wait_ge(x_copied, t + 1)
                        do(dve.tensor_tensor(heads(xd), heads(xtok), bc(dt[:, t, :], 2, HD), ALU.mult))
                        dve.tensor_tensor(heads(xdw[:]), heads(xd), bc(dlast[:, t, :], 2, HD), ALU.mult)
                        dve.tensor_copy(Btok[:], K.PS[:, 2, 0:256])
                        do(dve.tensor_copy(CB[:].rearrange("p g n -> p (g n)"), K.PS[:, 2, 256:512]))
                        dve.engine_nop().then_inc(dve_tok, 1)

                        def times_cb(hq):
                            dve.wait_ge(m_exp, 4 * t + hq + 1)
                            m = M[:, 4 * hq:4 * hq + 4, :]
                            dve.tensor_tensor(m, m, bc(CB[:, hq // 2, :], 1, 4), ALU.mult).then_inc(m_ready, 1)

                        for hq in range(4):
                            n = 4 * t + hq
                            dve.wait_ge(r_done, n + 1)
                            if n >= 2:
                                dve.wait_ge(m_exp, n - 1)
                            if hq == 0 and 1 <= t < NT:
                                dve.wait_ge(ehl_ready, t)
                            R = K.PS[:, 3 + hq % 2, :].rearrange("p (h n) -> p h n", h=4)
                            dve.tensor_copy(rl[:, 4 * hq:4 * hq + 4], R[:, :, P - 1])
                            dve.tensor_tensor(DD[:, hq % 2], R, bc(acs[:, t, 4 * hq:4 * hq + 4], 2, P),
                                              ALU.subtract).then_inc(r_read, 1)
                            dve.wait_ge(r_read, n + 1)
                            dve.tensor_tensor(DD[:, hq % 2], DD[:, hq % 2], bc(K.NM5[:, t, :], 1, 4),
                                              ALU.add).then_inc(d_ready, 1)
                            if hq:
                                times_cb(hq - 1)
                        times_cb(3)
                        dve.wait_ge(diag_done, t + 1)
                        dve.wait_ge(yd_ready, t + 1)
                        off = 1 <= t < NT
                        y = dve.tensor_tensor(Y[:, t, :], K.PSF[:, 2560:2560 + D], YD[:], ALU.add)
                        if off:
                            dve.wait_ge(off_done, t)
                            do(dve.tensor_tensor(heads(xd), heads(K.PSF[:, 0:D]), bc(eacs[:, t, :], 2, HD), ALU.mult))
                            y = dve.tensor_tensor(Y[:, t, :], Y[:, t, :], xd, ALU.add)
                        y.then_inc(y_done, 1)
                        if t < NT:
                            dve.wait_ge(s_done, t + 1)
                            if t == 0:
                                dve.tensor_copy(H[:], K.PSF[:, 1536:1536 + D]).then_inc(h_ready, 1)
                            else:
                                dve.wait_ge(ehl_ready, t + 1)
                                do(dve.tensor_tensor(heads(H[:]), heads(H[:]), bc(ehl[:], 2, HD), ALU.mult))
                                dve.tensor_tensor(H[:], H[:], K.PSF[:, 1536:1536 + D], ALU.add).then_inc(h_ready, 1)

        ssd_sample(nc, K, SX, Y, la, eacs, xdw, Btok, H, YD, XX)


def ssd_sample(nc, K, SX, Y, la, eacs, xdw, Btok, H, tmp, h0T):
    HP = SH // 2
    HB = NB // 2
    with ExitStack() as ctx:
        def sb(name, shape):
            return ctx.enter_context(nc.sbuf_tensor(name, shape, F32))

        low = K.YT[:, 0:KT, :].rearrange("p k n -> p (k n)")
        h0 = low[:, 0:HB * D].rearrange("p (b q n) -> p b q n", b=HB, q=HP)
        CTm = sb("e_CTm", [P, 2, NB, TS])
        Bm = sb("e_Bm", [TS, NB, 256])
        lax_ = low[0:TS, HB * D:HB * D + D]
        cdv = sb("e_cdv", [P, HP, NB])
        with stage(nc, "h0_in", "masked", "turned", "t_copied", "yoff_done", "cd_mm", "cd_ready", "s_mm", "s_read",
                   "h_new", "h_out", "hp_done", "dve_link") as (
                block, h0_in, masked, turned, t_copied, yoff_done, cd_mm, cd_ready, s_mm, s_read, h_new, h_out,
                hp_done, dve_link):
            def states(ap, half):
                return ap[half * HB:(half + 1) * HB].rearrange("b (q e) p n -> (e p) b q n", e=2)

            @block.scalar
            def _(act):
                for half in range(2):
                    if half:
                        act.wait_ge(h_out, 1)
                    for q in range(HP):
                        act.dma_start(h0[:, :, q, :], K.state_ssm[0, half * HB:(half + 1) * HB, 2 * q:2 * q + 2]
                                      .rearrange("b e p n -> (e p) b n")).then_inc(h0_in, 16)
                    if half == 0:
                        act.wait_ge(cd_mm, 1)
                        act.activation(cdv[:].rearrange("p q b -> p (q b)"), K.PS[:, 4, 0:HP * NB],
                                       ACT.Exp).then_inc(cd_ready, 1)
                    for b in range(HB * half, HB * half + HB):
                        act.wait_ge(turned, b + 1)
                        if b >= 2:
                            act.wait_ge(yoff_done, b - 1)
                        act.copy(h0T[:, b % 2, :], K.PSF[:, 0:D]).then_inc(t_copied, 1)

            @block.tensor
            def _(pe):
                pe.wait_ge(masked, 3)
                for q in range(HP):
                    last = pe.matmul(K.PS[:, 4, q * NB:(q + 1) * NB], lax_[:, q * P:(q + 1) * P], K.SELT[0:TS, :],
                                     start=True, stop=True)
                last.then_inc(cd_mm, 1)
                for half in range(2):
                    pe.wait_ge(h0_in, 16 * HP * (half + 1))
                    for b in range(HB * half, HB * half + HB):
                        if b:
                            pe.wait_ge(t_copied, b)
                        for q in range(HP):
                            last = pe.transpose(K.PSF[:, q * P:(q + 1) * P], h0[:, b - HB * half, q, :], K.ident[:])
                        last.then_inc(turned, 1)
                        pe.wait_ge(t_copied, b + 1)
                        for g in range(2):
                            last = pe.matmul(K.PS[0:TS, 2 + g, :], CTm[:, g, b, :], h0T[:, b % 2, g * 512:(g + 1) * 512],
                                             start=(b == 0), stop=(b == NB - 1))
                        last.then_inc(yoff_done, 1)
                    for q in range(HP):
                        n = half * HP + q
                        if n >= 3:
                            pe.wait_ge(s_read, n - 2)
                        g = q // (HP // 2)
                        pe.matmul(K.PS[:, 5 + n % 3, :], xdw[0:TS, q * P:(q + 1) * P],
                                  Bm[:, half * HB:(half + 1) * HB, g * P:(g + 1) * P], start=True, stop=True).then_inc(s_mm, 1)
                pe.wait_ge(t_copied, NB)
                for q in range(HP):
                    last = pe.transpose(K.PSF[:, q * P:(q + 1) * P], H[:, q * P:(q + 1) * P], K.ident[:])
                last.then_inc(hp_done, 1)

            @block.vector
            def _(dve):
                do = Chain(dve, dve_link)
                for g in range(2):
                    dve.tensor_tensor(CTm[:, g], bc(SX[:, 10 + g, SEQ:TOK], 1, NB), K.SELC[:], ALU.mult)
                dve.engine_nop().then_inc(masked, 1)
                dve.tensor_tensor(Bm[:], bc(Btok[0:TS, :], 1, NB), bc(K.SELT[0:TS, :], 2, 256), ALU.mult).then_inc(masked, 1)
                dve.tensor_copy(lax_.rearrange("p (h q) -> p h q", h=SH), bc(la[0:TS, NT, :], 2, HD)).then_inc(masked, 1)
                dve.wait_ge(cd_ready, 1)
                for half in range(2):
                    dve.wait_ge(turned, HB * (half + 1))
                    for q in range(HP):
                        n = half * HP + q
                        h = h0[:, :, q, :]
                        do(dve.tensor_tensor(h, h, bc(cdv[:, q, half * HB:(half + 1) * HB], 2, P), ALU.mult))
                        dve.wait_ge(s_mm, n + 1)
                        last = dve.tensor_tensor(h, h, K.PS[:, 5 + n % 3, :].rearrange("p (b n) -> p b n", b=HB), ALU.add)
                        last.then_inc(s_read, 1)
                dve.wait_ge(yoff_done, NB)
                do(dve.tensor_tensor(tmp[0:TS, :].rearrange("p (h q) -> p h q", h=SH),
                                     K.PSF[0:TS, D:2 * D].rearrange("p (h q) -> p h q", h=SH),
                                     bc(eacs[0:TS, NT, :], 2, HD), ALU.mult))
                dve.tensor_tensor(Y[0:TS, NT, :], Y[0:TS, NT, :], tmp[0:TS, :], ALU.add)
                dve.wait_ge(hp_done, 1)
                dve.wait_ge(t_copied, NB)
                dve.tensor_copy(h0T[:, 0, :], K.PSF[:, 0:D]).then_inc(h_new, 1)

            @block.sync
            def _(sp):
                for half in range(2):
                    sp.wait_ge(s_read, HP * (half + 1))
                    for q in range(HP):
                        sp.dma_start(K.o_ssm_s[0, half * HB:(half + 1) * HB, 2 * q:2 * q + 2]
                                     .rearrange("b e p n -> (e p) b n"), h0[:, :, q, :]).then_inc(K.state_out, 16)
                    K.n_state_out += HP
                    sp.wait_ge(K.state_out, 16 * K.n_state_out)
                    sp.sem_inc(h_out, 1)
                sp.wait_ge(h_new, 1)
                sp.dma_start(K.o_ssm_p[0, 0].rearrange("(q e) p n -> (e p) q n", e=2),
                             h0T[:, 0, :].rearrange("p (q n) -> p q n", q=HP)).then_inc(K.state_out, 16)
                K.n_state_out += 1
                sp.wait_ge(K.state_out, 16 * K.n_state_out)


def ssm_gate(nc, K, Y, chunk):
    with ExitStack() as ctx:
        SZ = ctx.enter_context(nc.sbuf_tensor("g_SZ", [P, 2, 512], F32))
        units = [(c, t) for c in range(2) for t in range(TT)]
        with stage(nc, "z_mm", "z_silu", "z_used") as (block, z_mm, z_silu, z_used):
            @block.sync
            def _(sp):
                fill_ring(K, sp, chunk + 1 + RING, z_mm, {chunk: TT, chunk + 1: 2 * TT})

            @block.tensor
            def _(pe):
                for i, (c, t) in enumerate(units):
                    if t == 0:
                        W = chunk_wait(K, pe, chunk + c)
                    if i >= 4:
                        pe.wait_ge(z_silu, i - 3)
                    proj_matmuls(K, pe, W, "N", t, i % 4).then_inc(z_mm, 1)

            @block.scalar
            def _(act):
                for i, (c, t) in enumerate(units):
                    n = TILES[t][1]
                    act.wait_ge(z_mm, i + 1)
                    if i >= 2:
                        act.wait_ge(z_used, i - 1)
                    act.activation(SZ[0:n, i % 2, :], K.PSF[0:n, (i % 4) * 1024:(i % 4) * 1024 + 512],
                                   ACT.Silu).then_inc(z_silu, 1)

            @block.vector
            def _(dve):
                for i, (c, t) in enumerate(units):
                    n = TILES[t][1]
                    y = Y[0:n, t, c * 512:(c + 1) * 512]
                    dve.wait_ge(z_silu, i + 1)
                    dve.tensor_tensor(y, y, SZ[0:n, i % 2, :], ALU.mult).then_inc(z_used, 1)


def ssm_norm(nc, K, Y):
    with ExitStack() as ctx:
        SQ = ctx.enter_context(nc.sbuf_tensor("n_sq", [P, D], F32))
        ss = ctx.enter_context(nc.sbuf_tensor("n_ss", [P, TT], F32))
        nw = ctx.enter_context(nc.sbuf_tensor("n_w", [P, KT], F32))
        with stage(nc, "sq_done", "rs_link", "rs_done", "h_ready", "t_done", "yt_copied", "nw_in") as (
                block, sq_done, rs_link, rs_done, h_ready, t_done, yt_copied, nw_in):
            @block.scalar
            def _(act):
                act.dma_start(nw[:], K.ssm_norm_w[0].rearrange("(k p) -> p k", p=P),
                              allow_slow_non_contiguous=True).then_inc(nw_in, 16)
                for t in range(TT):
                    if t:
                        act.wait_ge(sq_done, t)
                    act.activation(SQ[:], Y[:, t, :], ACT.Square, accum_out=ss[:, t:t + 1]).then_inc(sq_done, 1)
                inv_rms(act, K, ss[:], D, sq_done, TT, rs_link).then_inc(rs_done, 1)

            @block.vector
            def _(dve):
                dve.wait_ge(rs_done, 1)
                dve.wait_ge(nw_in, 16)
                for t in range(TT + 1):
                    if t < TT:
                        dve.tensor_scalar(Y[:, t, :], Y[:, t, :], ss[:, t:t + 1], None, ALU.mult).then_inc(h_ready, 1)
                    if t >= 1:
                        u = t - 1
                        dve.wait_ge(t_done, u + 1)
                        dve.tensor_tensor(K.YT[:, 0:8, u * P:(u + 1) * P],
                                          K.PSF[:, (u % 2) * D:(u % 2) * D + D].rearrange("p (k n) -> p k n", k=KT),
                                          bc(nw[:], 2, P), ALU.mult).then_inc(yt_copied, 1)

            @block.tensor
            def _(pe):
                for t in range(TT):
                    pe.wait_ge(h_ready, t + 1)
                    if t >= 2:
                        pe.wait_ge(yt_copied, t - 1)
                    for k in range(KT):
                        last = pe.transpose(K.PSF[:, (t % 2) * D + k * P:(t % 2) * D + (k + 1) * P],
                                            Y[:, t, k * P:(k + 1) * P], K.ident[:])
                    last.then_inc(t_done, 1)



SCALE = HD ** -0.5


def nsa(nc, K, chunk):
    with ExitStack() as ctx:
        def sb(name, shape):
            return ctx.enter_context(nc.sbuf_tensor(name, shape, F32))

        QT = sb("a_QT", [P, REP, TOK])
        KV = sb("a_KV", [P, TT, 768])
        GT = sb("a_GT", [P, TT, 3 * NH])
        KTT = sb("a_KTT", [P, 2, TOK])
        KCT = sb("a_KCT", [P, NBLK + NB * SBLK])
        VC = sb("a_VC", [NBLK, P])
        VCS = sb("a_VCS", [SBLK, NB, P])
        VCZ = sb("a_VCZ", [P, NH, HD])
        PCT = sb("a_PCT", [P, NT, P])
        GS = sb("a_GS", [P, NB, 3])

        def q_out(c):
            def evac(eng, pair, at):
                return copy_on(eng, in_halves(QT[:, 4 * c + at, :]), both_halves(K, pair))
            return evac

        def kv_out(eng, pair, t):
            n = TILES[t][1]
            return copy_on(eng, KV[0:n, t, 0:512], K.PSF[0:n, pair * 1024:pair * 1024 + 512])

        def win_out(eng, pair, t):
            n, o = TILES[t][1], pair * 1024
            copy_on(eng, KV[0:n, t, 512:768], K.PSF[0:n, o:o + 256])
            return eng.activation(GT[0:n, t, :], K.PSF[0:n, o + 256:o + 304], ACT.Sigmoid)

        units = []
        for c in range(2):
            for m in range(4):
                units.append((chunk + c, "T", m, 512, ("act", "dve")[m % 2], q_out(c)))
        for t in range(TT):
            units.append((chunk + 2, "N", t, 512, ("act", "dve")[t % 2], kv_out))
        for t in range(TT):
            units.append((chunk + 3, "N", t, 304, "act", win_out))
        project(nc, K, "nsa", units)
        nsa_compress(nc, K, chunk + 4, KV, KTT, KCT, VC, VCS, VCZ, GT, GS)
        nsa_compressed_scores(nc, K, QT, KCT, GT, PCT)
        nsa_prompt(nc, K, QT, KV, KTT, VCZ, PCT, GT)
        nsa_sample(nc, K, QT, KV, KTT, KCT, VCS, GS)


def nsa_compress(nc, K, chunk, KV, KTT, KCT, VC, VCS, VCZ, GT, GS):
    R = 2 * (NBLK + NB * SBLK)
    RG = R // 2
    PER = 6
    with ExitStack() as ctx:
        def sb(name, shape):
            return ctx.enter_context(nc.sbuf_tensor(name, shape, F32))

        rows = [K.HT[:].rearrange("p k n -> p (k n)")[:, 0:4096],
                K.YT[:, 8:16, :].rearrange("p k n -> p (k n)")[:, 0:4096]]
        FT = sb("b_FT", [P, 32, R])
        pe_rows = sb("b_pe", [32, 2, P])
        peT = sb("b_peT", [P, 2, 32])
        w2 = sb("b_w2", [P, 2, 2, HD])
        HS = sb("b_HS", [P, 2, 2, R])
        with stage(nc, "rows_in", "small_in", "pe_turned", "pe_copied", "turned", "t_copied", "hid_mm",
                   "hid_silu", "out_mm", "out_copied", "k_turned", "k_copied", "gates_out", "gates_in", "vcr_mm",
                   "dve_link") as (block, rows_in, small_in, pe_turned, pe_copied, turned, t_copied, hid_mm,
                                   hid_silu, out_mm, out_copied, k_turned, k_copied, gates_out, gates_in, vcr_mm,
                                   dve_link):
            groups = [list(range(a, min(a + PER, 32))) for a in range(0, 32, PER)]
            NG = len(groups)

            @block.sync
            def _(sp):
                sp.dma_start(K.o_nsa_kv_p[0, 0].rearrange("(t p) k g d -> p t (k g d)", p=P),
                             KV[:, 0:NT, 0:512]).then_inc(K.state_out, 16)
                sp.dma_start(K.o_nsa_kv_s[0].rearrange("b s k g d -> (b s) (k g d)"), KV[0:TS, NT, 0:512]).then_inc(K.state_out, 16)
                sp.dma_start(K.o_nsa_win_p[0, 0].rearrange("(t p) k g d -> p t (k g d)", p=P),
                             KV[:, 0:NT, 512:768]).then_inc(K.state_out, 16)
                for b in range(NB):
                    sp.dma_start(K.o_nsa_win_s[0, b, PAST - NS:].rearrange("s k g d -> s (k g d)"),
                                 KV[b * NS:(b + 1) * NS, NT, 512:768]).then_inc(K.state_out, 16)
                sp.wait_ge(K.past_in, 16 * NB * PAGES)
                K.n_state_out += 3 + NB
                sp.wait_ge(K.state_out, 16 * K.n_state_out)
                for kv in range(2):
                    for g in range(2):
                        c = kv * P + g * HD
                        sp.dma_start(rows[kv][g * RG:g * RG + NBLK].rearrange("p (s d) -> p s d", d=HD),
                                     K.o_nsa_kv_p[0, 0].rearrange("(n s) k g d -> n s (k g d)", s=HD)[:, :, c:c + HD])\
                          .then_inc(rows_in, 16)
                        sp.dma_start(rows[kv][g * RG + NBLK:(g + 1) * RG].rearrange("p (s d) -> p s d", d=HD),
                                     K.past.rearrange("b (n s) c -> (b n) s c", s=HD)[:, :, c:c + HD]).then_inc(rows_in, 16)
                fill_ring(K, sp, chunk + 3 + RING, hid_mm, {chunk: 1, chunk + 1: 2, chunk + 2: 3, chunk + 3: 4})

            @block.scalar
            def _(act):
                for kv, (pe_, w) in enumerate(((K.nsa_pe_k, K.nsa_ck_w2), (K.nsa_pe_v, K.nsa_cv_w2))):
                    act.dma_start(pe_rows[:, kv, :], pe_[0].rearrange("(k e) d -> k (e d)", e=2)).then_inc(small_in, 16)
                    act.dma_start(w2[:, kv], w[0].rearrange("(k p) n -> p k n", p=P)).then_inc(small_in, 16)
                act.dma_start(K.gate_rows, GT[0:TS, NT, :]).then_inc(gates_out, 16)
                act.wait_ge(gates_out, 16)
                for g in range(2):
                    for i in range(NS):
                        r = g * 64 + i * NS
                        for j in range(3):
                            src = K.gate_rows.rearrange("(b s) (j g m) -> s g j m b", s=NS, j=3, g=2)[i, g, j]
                            act.dma_start(GS[r:r + REP, :, j], src, allow_slow_non_contiguous=True).then_inc(gates_in, 16)
                for kv in range(2):
                    act.wait_ge(hid_mm, 2 * kv + 2)
                    for m in range(2):
                        act.activation(HS[:, kv, m, :], K.PS[:, 2 + m, 0:R], ACT.Silu).then_inc(hid_silu, 1)
                act.wait_ge(gates_in, 16 * 48)

            @block.tensor
            def _(pe):
                pe.wait_ge(small_in, 64)
                for kv in range(2):
                    last = pe.transpose(K.PS[:, 7, kv * 32:(kv + 1) * 32], pe_rows[:, kv, :], K.ident[0:32, 0:32])
                last.then_inc(pe_turned, 1)
                for j in range(2):
                    if j:
                        pe.wait_ge(k_copied, 1)
                    for t, n in TILES:
                        last = pe.transpose(K.PSF[:, 2048 + t * P:2048 + t * P + n],
                                            KV[0:n, t, 256 + 256 * j:384 + 256 * j], K.ident[0:n, 0:n])
                    last.then_inc(k_turned, 1)
                pe.wait_ge(rows_in, 16 * 8)
                for kv in range(2):
                    for n, ks in enumerate(groups):
                        i = kv * NG + n
                        if i >= 2:
                            pe.wait_ge(t_copied, i - 1)
                        for c, k in enumerate(ks):
                            last = pe.transpose(K.PS[:, i % 2, c * R:(c + 1) * R], rows[kv][0:R, k * P:(k + 1) * P],
                                                K.ident[0:R, 0:R])
                        last.then_inc(turned, 1)
                    if kv:
                        pe.wait_ge(hid_silu, 2)
                    for c in range(2):
                        W = chunk_wait(K, pe, chunk + 2 * kv + c).rearrange("p k (e n) -> p (k e) n", e=2)
                        for k in range(16 * c, 16 * c + 16):
                            if k % PER == 0 or k == 16 * c:
                                pe.wait_ge(t_copied, kv * NG + k // PER + 1)
                            for m in range(2):
                                last = pe.matmul(K.PS[:, 2 + m, 0:R], W[:, k - 16 * c, m * P:(m + 1) * P], FT[:, k, :],
                                                 start=(k == 0), stop=(k == 31))
                        last.then_inc(hid_mm, 1)
                    pe.wait_ge(hid_silu, 2 * kv + 2)
                    if kv == 0:
                        pe.wait_ge(k_copied, 2)
                        for g in range(2):
                            for k in range(2):
                                last = pe.matmul(K.PS[g * HD:(g + 1) * HD, 4, 0:RG], w2[:, 0, k, :],
                                                 HS[:, 0, k, g * RG:(g + 1) * RG], start=(k == 0), stop=(k == 1))
                        last.then_inc(out_mm, 1)
                    else:
                        for g in range(2):
                            for k in range(2):
                                pe.matmul(K.PS[0:NBLK, 5, g * HD:(g + 1) * HD], HS[:, 1, k, g * RG:g * RG + NBLK],
                                          w2[:, 1, k, :], start=(k == 0), stop=(k == 1))
                            for b in range(NB):
                                r = g * RG + NBLK + SBLK * b
                                o = 3072 + b * P + g * HD
                                for k in range(2):
                                    last = pe.matmul(K.PSF[0:SBLK, o:o + HD], HS[:, 1, k, r:r + SBLK], w2[:, 1, k, :],
                                                     start=(k == 0), stop=(k == 1))
                        last.then_inc(out_mm, 1)
                pe.wait_ge(out_copied, 3)
                pe.matmul(K.PS[:, 0, 0:P], K.R8[:], VC[:], start=True, stop=True).then_inc(vcr_mm, 1)

            @block.vector
            def _(dve):
                dve.wait_ge(pe_turned, 1)
                dve.tensor_copy(peT[:].rearrange("p a k -> p (a k)"), K.PS[:, 7, 0:64]).then_inc(pe_copied, 1)
                for j in range(2):
                    dve.wait_ge(k_turned, j + 1)
                    dve.tensor_copy(KTT[:, j, :], K.PSF[:, 2048:2048 + TOK]).then_inc(k_copied, 1)
                dve.wait_ge(pe_copied, 1)
                for kv in range(2):
                    if kv:
                        dve.wait_ge(hid_mm, 2)
                    for n, ks in enumerate(groups):
                        i = kv * NG + n
                        m = len(ks)
                        dve.wait_ge(turned, i + 1)
                        dve.tensor_tensor(FT[:, ks[0]:ks[0] + m, :],
                                          K.PS[:, i % 2, 0:m * R].rearrange("p (k r) -> p k r", r=R),
                                          bc(peT[:, kv, ks[0]:ks[0] + m], 2, R), ALU.add).then_inc(t_copied, 1)
                    dve.wait_ge(out_mm, kv + 1)
                    if kv == 0:
                        dve.tensor_copy(KCT[:], K.PS[:, 4, 0:RG]).then_inc(out_copied, 1)
                dve.tensor_copy(VC[:], K.PS[0:NBLK, 5, 0:P]).then_inc(out_copied, 1)
                dve.tensor_copy(VCS[:].rearrange("p b c -> p (b c)"), K.PSF[0:SBLK, 3072:4096]).then_inc(out_copied, 1)
                dve.wait_ge(vcr_mm, 1)
                for g in range(2):
                    dve.tensor_tensor(VCZ[:, REP * g:REP * (g + 1), :], bc(K.PS[:, 0, g * HD:(g + 1) * HD], 1, REP),
                                      bc(K.SELH[:, REP * g:REP * (g + 1)], 2, HD), ALU.mult)


def nsa_compressed_scores(nc, K, QT, KCT, GT, PCT):
    with ExitStack() as ctx:
        def sb(name, shape):
            return ctx.enter_context(nc.sbuf_tensor(name, shape, F32))

        S = sb("c_S", [P, NT, NH, NBLK])
        mx = sb("c_mx", [P, NT, NH])
        sm = sb("c_sm", [P, NT, NH])
        with stage(nc, "s_mm", "s_ready", "exp_done", "p_ready", "turned", "dve_link") as (
                block, s_mm, s_ready, exp_done, p_ready, turned, dve_link):
            flat = S[:].rearrange("p t h n -> p (t h) n")
            m2, s2 = mx[:].rearrange("p t h -> p (t h)"), sm[:].rearrange("p t h -> p (t h)")

            @block.tensor
            def _(pe):
                for t in range(NT):
                    for h in range(NH):
                        g, m = h // REP, h % REP
                        o = (t * REP + m) * NBLK
                        last = pe.matmul(K.PS[:, g, o:o + NBLK], QT[g * HD:(g + 1) * HD, m, t * P:(t + 1) * P],
                                         KCT[g * HD:(g + 1) * HD, 0:NBLK], start=True, stop=True)
                last.then_inc(s_mm, 1)
                pe.wait_ge(p_ready, 1)
                for t in range(NT):
                    last = pe.transpose(K.PS[:, 2, t * P:(t + 1) * P], S[:, t].rearrange("p h n -> p (h n)"), K.ident[:])
                last.then_inc(turned, 1)

            @block.scalar
            def _(act):
                act.wait_ge(s_ready, 1)
                act.activation(flat, flat, ACT.Exp, scale=SCALE).then_inc(exp_done, 1)

            @block.vector
            def _(dve):
                do = Chain(dve, dve_link)
                dve.wait_ge(s_mm, 1)
                for g in range(2):
                    ps = K.PS[:, g, 0:256].rearrange("p (t m n) -> p t m n", t=NT, m=REP)
                    for t in range(NT):
                        do(dve.tensor_tensor(S[:, t, g * REP:(g + 1) * REP], ps[:, t], bc(K.CN[:, t, :], 1, REP), ALU.add))
                do(dve.tensor_reduce(m2, flat, AX.X, ALU.max))
                dve.tensor_tensor(flat, flat, bc(m2, 2, NBLK), ALU.subtract).then_inc(s_ready, 1)
                dve.wait_ge(exp_done, 1)
                do(dve.tensor_reduce(s2, flat, AX.X, ALU.add))
                do(dve.reciprocal(s2, s2))
                do(dve.tensor_tensor(sm[:], sm[:], GT[:, 0:NT, 0:NH], ALU.mult))
                do(dve.tensor_tensor(flat, flat, bc(s2, 2, NBLK), ALU.mult))
                for t in range(NT):
                    do(dve.tensor_tensor(S[:, t], S[:, t], bc(K.CV[:, t, :], 1, NH), ALU.mult))
                dve.engine_nop().then_inc(p_ready, 1)
                dve.wait_ge(turned, 1)
                dve.tensor_copy(PCT[:].rearrange("p t n -> p (t n)"), K.PS[:, 2, :])


def nsa_prompt(nc, K, QT, KV, KTT, VCZ, PCT, GT):
    units = [(m, g, i) for m in range(REP) for g in range(2) for i in range(NT)]
    N = len(units)
    with ExitStack() as ctx:
        def sb(name, shape):
            return ctx.enter_context(nc.sbuf_tensor(name, shape, F32))

        E = sb("p_E", [P, 3, 2, SEQ])
        PT = sb("p_PT", [P, 2, 2, NT, P])
        mx = sb("p_mx", [P, 3, 2])
        sm = sb("p_sm", [P, 3, 2])
        with stage(nc, "s_mm", "nm_ready", "exp_done", "rg_ready", "p_sel", "p_win", "turned", "t_act", "t_dve", "pv_done",
                   "y_out", "dve_link") as (block, s_mm, nm_ready, exp_done, rg_ready, p_sel, p_win, turned, t_act, t_dve,
                                            pv_done, y_out, dve_link):
            @block.sync
            def _(sp):
                sp.dma_start(K.o_nsa_win_s[0, :, 0:PAST - NS].rearrange("b r k g d -> b r (k g d)"),
                             K.nsa_win[0, :, NS:].rearrange("b r k g d -> b r (k g d)")).then_inc(K.kept, 16)
                for o, c, w in ((K.o_dil_s[0], K.dil[0], 128), (K.o_dil_s[1], K.dil[1], PAST),
                                (K.o_dil_s[2], K.dil[2], PAST)):
                    sp.dma_start(o[0, :, 0:w - NS].rearrange("b r k h d -> b r (k h d)"),
                                 c[0, :, NS:].rearrange("b r k h d -> b r (k h d)")).then_inc(K.kept, 16)

            @block.tensor
            def _(pe):
                def scores(u):
                    m, g, i = units[u]
                    r = slice(g * HD, (g + 1) * HD)
                    if u >= 2:
                        pe.wait_ge(exp_done, 2 * (u - 1))
                    for j in range(2):
                        last = pe.matmul(K.PS[:, 2 * (u % 2) + j, 0:(i + 1) * P], QT[r, m, i * P:(i + 1) * P],
                                         KTT[r, j, 0:(i + 1) * P], start=True, stop=True)
                    last.then_inc(s_mm, 1)

                def turn(u):
                    i = units[u][2]
                    pe.wait_ge(p_sel, u + 1)
                    pe.wait_ge(p_win, u + 1)
                    if u:
                        pe.wait_ge(t_act, u)
                        pe.wait_ge(t_dve, u)
                    for j in range(2):
                        for k in range(i + 1):
                            last = pe.transpose(K.PS[:, 4 + j, k * P:(k + 1) * P], E[:, u % 3, j, k * P:(k + 1) * P], K.ident[:])
                    last.then_inc(turned, 1)

                def values(u):
                    m, g, i = units[u]
                    n = u // NT
                    out = K.PS[g * HD:(g + 1) * HD, 6 + n % 2, :]
                    if i == 0:
                        if n >= 2:
                            pe.wait_ge(y_out, n - 1)
                        pe.matmul(out, VCZ[:, g * REP + m, :], PCT[:].rearrange("p t n -> p (t n)"), start=True, stop=False,
                                  skip_group_check=True)
                    pe.wait_ge(t_act, u + 1)
                    pe.wait_ge(t_dve, u + 1)
                    for j in range(2):
                        for k in range(i + 1):
                            c = 384 + 256 * j + g * HD
                            last = pe.matmul(out[:, i * P:(i + 1) * P], KV[:, k, c:c + HD], PT[:, u % 2, j, k, :],
                                             start=False, stop=(i == NT - 1 and j == 1 and k == i), skip_group_check=True)
                    last.then_inc(pv_done, 1)

                for s in range(N + 3):
                    if s < N:
                        scores(s)
                    if 2 <= s < N + 2:
                        turn(s - 2)
                    if s >= 3:
                        values(s - 3)

            @block.scalar
            def _(act):
                def evacuate(u):
                    i = units[u][2]
                    act.wait_ge(turned, u + 1)
                    if u >= 2:
                        act.wait_ge(pv_done, u - 1)
                    act.copy(PT[:, u % 2, 0, 0:i + 1, :].rearrange("p k n -> p (k n)"), K.PS[:, 4, 0:(i + 1) * P]).then_inc(t_act, 1)

                for u in range(N):
                    if u >= 3:
                        evacuate(u - 3)
                    L = (units[u][2] + 1) * P
                    act.wait_ge(nm_ready, u + 1)
                    if u >= 3:
                        act.wait_ge(turned, u - 2)
                        act.wait_ge(rg_ready, u - 2)
                    for j in range(2):
                        act.activation(E[:, u % 3, j, 0:L], K.PS[:, 2 * (u % 2) + j, 0:L], ACT.Exp, scale=SCALE,
                                       bias=mx[:, u % 3, j:j + 1], accum_out=sm[:, u % 3, j:j + 1]).then_inc(exp_done, 1)
                for u in range(N - 3, N):
                    evacuate(u)

            @block.gpsimd
            def _(pool):
                for u in range(N):
                    L = (units[u][2] + 1) * P
                    pool.wait_ge(rg_ready, u + 1)
                    pool.tensor_scalar(E[:, u % 3, 0, 0:L], E[:, u % 3, 0, 0:L], sm[:, u % 3, 0:1], None,
                                       ALU.mult).then_inc(p_sel, 1)

            @block.vector
            def _(dve):
                do = Chain(dve, dve_link)

                def front(u):
                    i = units[u][2]
                    L = (i + 1) * P
                    b = 2 * (u % 2)
                    dve.wait_ge(s_mm, u + 1)
                    if u >= 3:
                        dve.wait_ge(exp_done, 2 * (u - 2))
                    diag = K.PS[:, b:b + 2, i * P:L]
                    do(dve.tensor_tensor(diag, diag, bc(K.CM[:], 1, 2), ALU.add))
                    do(dve.tensor_reduce(mx[:, u % 3, :], K.PS[:, b:b + 2, 0:L], AX.X, ALU.max))
                    dve.tensor_scalar(mx[:, u % 3, :], mx[:, u % 3, :], -SCALE, None, ALU.mult).then_inc(nm_ready, 1)

                def back(u):
                    m, g, i = units[u]
                    h = g * REP + m
                    dve.wait_ge(exp_done, 2 * (u + 1))
                    do(dve.reciprocal(sm[:, u % 3, :], sm[:, u % 3, :]))
                    dve.tensor_tensor(sm[:, u % 3, :], sm[:, u % 3, :],
                                      GT[:, i, :].rearrange("p (j h) -> p j h", j=3)[:, 1:3, h], ALU.mult).then_inc(rg_ready, 1)
                    dve.wait_ge(rg_ready, u + 1)
                    L = (i + 1) * P
                    dve.tensor_scalar(E[:, u % 3, 1, 0:L], E[:, u % 3, 1, 0:L], sm[:, u % 3, 1:2], None, ALU.mult).then_inc(p_win, 1)

                def evacuate(u):
                    m, g, i = units[u]
                    dve.wait_ge(turned, u + 1)
                    if u >= 2:
                        dve.wait_ge(pv_done, u - 1)
                    dve.tensor_copy(PT[:, u % 2, 1, 0:i + 1, :].rearrange("p k n -> p (k n)"), K.PS[:, 5, 0:(i + 1) * P]).then_inc(t_dve, 1)

                def y(n):
                    m, g, _ = units[n * NT]
                    r = slice(g * HD, (g + 1) * HD)
                    dve.wait_ge(pv_done, (n + 1) * NT)
                    dve.tensor_copy(K.YT[r, 8 + m, 0:SEQ], K.PS[r, 6 + n % 2, :]).then_inc(y_out, 1)

                for s in range(N + 3):
                    if s >= 3:
                        evacuate(s - 3)
                    if s < N:
                        front(s)
                    if 1 <= s <= N:
                        back(s - 1)
                    if s >= 8 and (s - 8) % NT == 0:
                        y((s - 8) // NT)
                y(N // NT - 1)


def nsa_sample(nc, K, QT, KV, KTT, KCT, VCS, GS):
    NK = PAST + TS
    with ExitStack() as ctx:
        def sb(name, shape):
            return ctx.enter_context(nc.sbuf_tensor(name, shape, F32))

        old = sb("q_old", [P, 2, 2, PAGES, 256])
        KTb = sb("q_KTb", [P, 2, 4, P])
        Qz = sb("q_Qz", [P, 2, P])
        E = sb("q_E", [P, 2, NK])
        Ec = sb("q_Ec", [P, SBLK])
        PTa = sb("q_PTa", [P, 4, P])
        PTb = sb("q_PTb", [TS, 2, P])
        PTc = sb("q_PTc", [SBLK, P])
        mx = sb("q_mx", [P, 3])
        sm = sb("q_sm", [P, 3])
        with stage(nc, "old_in", "old_in_odd", "zeroed", "k_turned", "q_ready", "s_mm", "nm_ready", "exp_done", "p_ready", "turned",
                   "t_copied", "pv_done", "y_out", "dve_link") as (
                block, old_in, old_in_odd, zeroed, k_turned, q_ready, s_mm, nm_ready, exp_done, p_ready, turned, t_copied,
                pv_done, y_out, dve_link):
            @block.sync
            def _(sp):
                for b in range(NB):
                    if b >= 2:
                        sp.wait_ge(pv_done, b - 1)
                    s = (old_in, old_in_odd)[b % 2]
                    sp.dma_start(old[:, b % 2, 0], K.past[b, :, 256:512].rearrange("(n p) c -> p n c", p=P)).then_inc(s, 16)
                    sp.dma_start(old[:, b % 2, 1], K.nsa_win[0, b].rearrange("(n p) k g d -> p n (k g d)", p=P)).then_inc(s, 16)

            @block.gpsimd
            def _(pool):
                pool.memset(Qz[:], 0.0).then_inc(zeroed, 1)

            @block.tensor
            def _(pe):
                def turn_keys(b):
                    pe.wait_ge((old_in, old_in_odd)[b % 2], 32 * (b // 2 + 1))
                    if b:
                        pe.wait_ge(q_ready, b)
                    for j in range(2):
                        for n in range(PAGES):
                            last = pe.transpose(K.PS[:, 0, (2 * j + n) * P:(2 * j + n + 1) * P],
                                                old[:, b % 2, j, n, 0:P], K.ident[:])
                    last.then_inc(k_turned, 1)

                turn_keys(0)
                for b in range(NB):
                    pe.wait_ge(q_ready, b + 1)
                    if b:
                        pe.wait_ge(exp_done, 3 * b)
                    for j in range(2):
                        pe.matmul(K.PS[:, 1 + j, 0:PAST], Qz[:, b % 2, :],
                                  KTb[:, b % 2, 2 * j:2 * j + 2, :].rearrange("p n c -> p (n c)"), start=True, stop=True)
                        last = pe.matmul(K.PS[:, 1 + j, PAST:NK], Qz[:, b % 2, :], KTT[:, j, SEQ:TOK], start=True, stop=True)
                    last = pe.matmul(K.PS[:, 1, NK:NK + SBLK], Qz[:, b % 2, :], KCT[:, NBLK + SBLK * b:NBLK + SBLK * (b + 1)],
                                     start=True, stop=True)
                    last.then_inc(s_mm, 1)
                    if b + 1 < NB:
                        turn_keys(b + 1)
                    pe.wait_ge(p_ready, b + 1)
                    if b:
                        pe.wait_ge(t_copied, 3 * b)
                    for j in range(2):
                        for n in range(2):
                            pe.transpose(K.PS[:, 4, (2 * j + n) * P:(2 * j + n + 1) * P], E[:, j, n * P:(n + 1) * P], K.ident[:])
                        pe.transpose(K.PS[0:TS, 5, j * P:(j + 1) * P], E[:, j, PAST:NK], K.ident[:])
                    pe.transpose(K.PS[0:SBLK, 5, 256:256 + P], Ec[:], K.ident[:]).then_inc(turned, 1)
                    pe.wait_ge(t_copied, 3 * (b + 1))
                    if b:
                        pe.wait_ge(y_out, b)
                    for j in range(2):
                        for n in range(2):
                            pe.matmul(K.PS[:, 6, 0:P], old[:, b % 2, j, n, P:256], PTa[:, 2 * j + n, :],
                                      start=(j == 0 and n == 0), stop=False)
                        c = 384 + 256 * j
                        pe.matmul(K.PS[:, 6, 0:P], KV[0:TS, NT, c:c + P], PTb[:, j, :], start=False, stop=False)
                    pe.matmul(K.PS[:, 6, 0:P], VCS[:, b, :], PTc[:], start=False, stop=True).then_inc(pv_done, 1)

            @block.scalar
            def _(act):
                for b in range(NB):
                    act.wait_ge(nm_ready, b + 1)
                    if b:
                        act.wait_ge(turned, b)
                    for j in range(2):
                        act.activation(E[:, j, :], K.PS[:, 1 + j, 0:NK], ACT.Exp, scale=SCALE, bias=mx[:, j:j + 1],
                                       accum_out=sm[:, j:j + 1]).then_inc(exp_done, 1)
                    act.activation(Ec[:], K.PS[:, 1, NK:NK + SBLK], ACT.Exp, scale=SCALE, bias=mx[:, 2:3],
                                   accum_out=sm[:, 2:3]).then_inc(exp_done, 1)

            @block.vector
            def _(dve):
                do = Chain(dve, dve_link)
                dve.wait_ge(zeroed, 1)

                def keys(b):
                    dve.wait_ge(k_turned, b + 1)
                    do(dve.tensor_copy(KTb[:, b % 2].rearrange("p n c -> p (n c)"), K.PS[:, 0, :]))
                    for g in range(2):
                        r = slice(g * HD, (g + 1) * HD)
                        t0 = SEQ + b * NS
                        last = dve.tensor_copy(Qz[r, b % 2, g * HD:(g + 1) * HD].rearrange("p (i m) -> p i m", i=NS),
                                               QT[r, :, t0:t0 + NS].rearrange("p m i -> p i m"))
                    last.then_inc(q_ready, 1)

                keys(0)
                for b in range(NB):
                    dve.wait_ge(s_mm, b + 1)
                    new = K.PS[:, 1:3, PAST:NK]
                    mask = K.MO[:, 0].rearrange("p a s -> p (a s)")[:, (7 - b) * NS:(7 - b) * NS + TS]
                    do(dve.tensor_tensor(new, new, bc(mask, 1, 2), ALU.add))
                    do(dve.tensor_reduce(mx[:, 0:2], K.PS[:, 1:3, 0:NK], AX.X, ALU.max))
                    do(dve.tensor_reduce(mx[:, 2:3], K.PS[:, 1, NK:NK + SBLK], AX.X, ALU.max))
                    dve.tensor_scalar(mx[:], mx[:], -SCALE, None, ALU.mult).then_inc(nm_ready, 1)
                    if b + 1 < NB:
                        keys(b + 1)
                    dve.wait_ge(exp_done, 3 * (b + 1))
                    do(dve.reciprocal(sm[:], sm[:]))
                    do(dve.tensor_tensor(sm[:, 0:2], sm[:, 0:2], GS[:, b, 1:3], ALU.mult))
                    do(dve.tensor_tensor(sm[:, 2:3], sm[:, 2:3], GS[:, b, 0:1], ALU.mult))
                    dve.tensor_tensor(E[:], E[:], bc(sm[:, 0:2], 2, NK), ALU.mult)
                    dve.tensor_scalar(Ec[:], Ec[:], sm[:, 2:3], None, ALU.mult).then_inc(p_ready, 1)
                    dve.wait_ge(turned, b + 1)
                    if b:
                        dve.wait_ge(pv_done, b)
                    dve.tensor_copy(PTa[:].rearrange("p n c -> p (n c)"), K.PS[:, 4, :]).then_inc(t_copied, 1)
                    dve.tensor_copy(PTb[:].rearrange("p n c -> p (n c)"), K.PS[0:TS, 5, 0:256]).then_inc(t_copied, 1)
                    dve.tensor_copy(PTc[:], K.PS[0:SBLK, 5, 256:256 + P]).then_inc(t_copied, 1)
                    dve.wait_ge(pv_done, b + 1)
                    for g in range(2):
                        r = slice(g * HD, (g + 1) * HD)
                        t0 = SEQ + b * NS
                        last = dve.tensor_copy(K.YT[r, 8:16, t0:t0 + NS].rearrange("p m i -> p i m"),
                                               K.PS[r, 6, g * HD:(g + 1) * HD].rearrange("p (i m) -> p i m", i=NS))
                    last.then_inc(y_out, 1)



def split_products(pe, out, terms):
    n = 0
    for (ah, al), (bh, bl) in terms:
        for a, b in ((ah, bh), (ah, bl), (al, bh)):
            last = pe.matmul(out, a, b, start=(n == 0), stop=(n == 3 * len(terms) - 1))
            n += 1
    return last


def split_chunk(K, act, n, WH, i, hi_done, kt=8):
    act.wait_ge(K.w_landed[n % RING], 16 * sum(len(K.chunks[m]) for m in range(n % RING, n + 1, RING)))
    act.copy(WH[:, i % 2, 0:kt], K.WR[:, n % RING, 0:kt]).then_inc(hi_done, 1)


def low_chunk(K, pool, n, WH, i, hi_done, lo_done, kt=8):
    pool.wait_ge(hi_done, i + 1)
    pool.tensor_tensor(K.WRr[:, n % RING, 0:kt], K.WR[:, n % RING, 0:kt], WH[:, i % 2, 0:kt].bitcast(F32),
                       ALU.subtract).then_inc(lo_done, 1)


def project_out(nc, K, name, chunk, parts, post_w):
    NC = len(parts)
    NA = sum(parts)
    with ExitStack() as ctx:
        AH = ctx.enter_context(nc.sbuf_tensor(f"{name}_AH", [P, NA, TOK], F32R))
        WH = ctx.enter_context(nc.sbuf_tensor(f"{name}_WH", [P, 2, 8, 512], F32R))
        PW = ctx.enter_context(nc.sbuf_tensor(f"{name}_pw", [P, D], F32))
        ss = ctx.enter_context(nc.sbuf_tensor(f"{name}_ss", [P, TT], F32))
        MO = K.HT[:].rearrange("p k n -> p (k n)").rearrange("p (t d) -> p t d", t=TT)
        with stage(nc, "w_in", "hi_done", "lo_done", "a_high", "a_low", "mm_done", "e_act", "e_dve", "sq_done", "rs_link",
                   "rs_done", "scaled", "zeroed", "x_done") as (
                block, w_in, hi_done, lo_done, a_high, a_low, mm_done, e_act, e_dve, sq_done, rs_link, rs_done, scaled,
                zeroed, x_done):
            n_act, n_dve = TT - TT // 2, TT // 2

            @block.sync
            def _(sp):
                sp.dma_start(PW[:], post_w.partition_broadcast(P)).then_inc(w_in, 16)
                fill_ring(K, sp, chunk + 2 * NC - 1 + RING, mm_done, {chunk + i: TT * (i + 1) for i in range(2 * NC)})

            @block.gpsimd
            def _(pool):
                pool.memset(ss[:], 1.0).then_inc(zeroed, 1)
                for i in range(2 * NC):
                    low_chunk(K, pool, chunk + i, WH, i, hi_done, lo_done, parts[i % NC])

            @block.tensor
            def _(pe):
                for half in range(2):
                    k0 = 0
                    for c, kt in enumerate(parts):
                        i = half * NC + c
                        pe.wait_ge(hi_done, i + 1)
                        pe.wait_ge(lo_done, i + 1)
                        pe.wait_ge(a_high, k0 + kt)
                        pe.wait_ge(a_low, k0 + kt)
                        WL = K.WRr[:, (chunk + i) % RING]
                        for t, n in TILES:
                            bank = (half * TT + t) % 8
                            if half and c == 0 and bank < 2:
                                pe.wait_ge(e_act, 1)
                                pe.wait_ge(e_dve, 1)
                            x = slice(t * P, t * P + n)
                            for k in range(kt):
                                ah, al, wh, wl = AH[:, k0 + k, x], K.YTr[:, k0 + k, x], WH[:, i % 2, k, :], WL[:, k, :]
                                for m, (a, w) in enumerate(((ah, wh), (ah, wl), (al, wh))):
                                    last = pe.matmul(K.PS[0:n, bank, :], a, w, start=(c == 0 and k == 0 and m == 0),
                                                     stop=(c == NC - 1 and k == kt - 1 and m == 2))
                            last.then_inc(mm_done, 1)
                        k0 += kt

            def evacuate(eng, sem, half, t):
                n = TILES[t][1]
                eng.wait_ge(mm_done, ((half + 1) * NC - 1) * TT + t + 1)
                copy_on(eng, MO[0:n, t, half * 512:(half + 1) * 512], K.PS[0:n, (half * TT + t) % 8, :]).then_inc(sem, 1)

            @block.scalar
            def _(act):
                k0 = 0
                for i, kt in enumerate(parts):
                    split_chunk(K, act, chunk + i, WH, i, hi_done, kt)
                    for k in range(k0, k0 + kt):
                        act.copy(AH[:, k, :], K.YT[:, k, 0:TOK]).then_inc(a_high, 1)
                    k0 += kt
                act.wait_ge(mm_done, TT)
                split_chunk(K, act, chunk + 2, WH, 2, hi_done, parts[0])
                for half in range(2):
                    for t in range(0, TT, 2):
                        evacuate(act, e_act, half, t)
                    if half == 0:
                        act.wait_ge(mm_done, 2 * TT)
                        split_chunk(K, act, chunk + 3, WH, 3, hi_done, parts[1])
                act.wait_ge(zeroed, 1)
                for t, n in TILES:
                    act.wait_ge(e_act, 2 * n_act)
                    act.wait_ge(e_dve, 2 * n_dve)
                    if t:
                        act.wait_ge(sq_done, t)
                    act.activation(K.PSF[0:n, 0:D], MO[0:n, t, :], ACT.Square, accum_out=ss[0:n, t:t + 1]).then_inc(sq_done, 1)
                inv_rms(act, K, ss[:], D, sq_done, TT, rs_link).then_inc(rs_done, 1)

            @block.vector
            def _(dve):
                for k in range(NA):
                    dve.wait_ge(a_high, k + 1)
                    dve.tensor_tensor(K.YTr[:, k, 0:TOK], K.YT[:, k, 0:TOK], AH[:, k, :].bitcast(F32), ALU.subtract).then_inc(a_low, 1)
                for half in range(2):
                    for t in range(1, TT, 2):
                        evacuate(dve, e_dve, half, t)
                dve.wait_ge(rs_done, 1)
                dve.wait_ge(w_in, 16)
                for t, n in TILES:
                    dve.scalar_tensor_tensor(MO[0:n, t, :], MO[0:n, t, :], ss[0:n, t:t + 1], PW[0:n, :], ALU.mult,
                                             ALU.mult).then_inc(scaled, 1)
                    dve.wait_ge(scaled, t + 1)
                    dve.tensor_tensor(K.X[0:n, t, :], K.X[0:n, t, :], MO[0:n, t, :], ALU.add).then_inc(x_done, 1)


MLP_ROUNDS = HID // 512


def mlp_order():
    order = [(True, 0)]
    for r in range(1, MLP_ROUNDS):
        order += [(True, r), (False, r - 1)]
    return order + [(False, MLP_ROUNDS - 1)]


def mlp(nc, K, layer, chunk, out=None):
    order = mlp_order()
    with ExitStack() as ctx:
        def sb(name, shape, dt=F32):
            return ctx.enter_context(nc.sbuf_tensor(f"mlp{layer}_{name}", shape, dt))

        HH = sb("HH", [P, KT, TP], F32R)
        WH = sb("WH", [P, 2, 8, 512], F32R)
        norm_transpose(nc, K, 2 * layer + 1, HH)
        ACC = sb("ACC", [P, TT, D])
        PW = sb("PW", [P, D])
        ss = sb("ss", [P, TT])
        HL = K.HTr

        def hidden(r, j):
            o = 8 * (r % 2) + j
            return K.YTr[:, o, 0:TOK], K.YTr[:, o + 4, 0:TOK]

        def whole(r, j):
            return K.YT[:, 8 * (r % 2) + j + 4, 0:TOK]

        with stage(nc, "hi_done", "lo_done", "up_mm", "down_mm", "relu_done", "sq_done", "high_done", "low_done",
                   "acc_done") as (block, hi_done, lo_done, up_mm, down_mm, relu_done, sq_done, high_done, low_done,
                                   acc_done):
            def last_use(i):
                up, r = order[i]
                return (up_mm, 4 * (r + 1)) if up else (down_mm, 2 * TT * (r + 1))

            @block.sync
            def _(sp):
                sp.dma_start(PW[:], K.norm_mlp_post[layer].partition_broadcast(P)).then_inc(K.weights_in, 16)
                K.n_weights_in += 1
                fill_ring(K, sp, chunk + len(order) - 1 + RING, None, {chunk + i: last_use(i) for i in range(len(order))})

            @block.tensor
            def _(pe):
                for i, (up, r) in enumerate(order):
                    pe.wait_ge(hi_done, i + 1)
                    pe.wait_ge(lo_done, i + 1)
                    wh, wl = WH[:, i % 2], K.WRr[:, (chunk + i) % RING]
                    if up:
                        for j in range(4):
                            u = 4 * r + j
                            if u >= 2:
                                pe.wait_ge(relu_done, u - 1)
                            c = slice(j * P, (j + 1) * P)
                            for b in range(2):
                                x = slice(b * HALF, (b + 1) * HALF)
                                last = split_products(pe, K.PS[:, 2 * (u % 2) + b, 0:HALF],
                                                [((wh[:, k, c], wl[:, k, c]), (HH[:, k, x], HL[:, k, x])) for k in range(KT)])
                            last.then_inc(up_mm, 1)
                    else:
                        pe.wait_ge(high_done, 4 * (r + 1))
                        pe.wait_ge(low_done, 4 * (r + 1))
                        wh4, wl4 = (w.rearrange("p (k h) n -> p k (h n)", h=2) for w in (wh, wl))
                        for t, n in TILES:
                            for half in range(2):
                                v = (r * TT + t) * 2 + half
                                if v >= 4:
                                    pe.wait_ge(acc_done, v - 3)
                                x, w = slice(t * P, t * P + n), slice(half * 512, (half + 1) * 512)
                                last = split_products(pe, K.PS[0:n, 4 + v % 4, :],
                                                [(tuple(a[:, x] for a in hidden(r, j)), (wh4[:, j, w], wl4[:, j, w]))
                                                 for j in range(4)])
                                last.then_inc(down_mm, 1)

            @block.scalar
            def _(act):
                def split(i):
                    if i >= 2:
                        act.wait_ge(*last_use(i - 2))
                    split_chunk(K, act, chunk + i, WH, i, hi_done)

                split(0)
                for i, (up, r) in enumerate(order):
                    if i + 1 < len(order):
                        split(i + 1)
                    if up:
                        for j in range(4):
                            u = 4 * r + j
                            act.wait_ge(up_mm, u + 1)
                            if u >= 8:
                                act.wait_ge(down_mm, 2 * TT * (r - 1))
                            act.activation(in_halves(whole(r, j)), both_halves(K, u % 2), ACT.Relu).then_inc(relu_done, 1)

            @block.gpsimd
            def _(pool):
                for i in range(len(order)):
                    low_chunk(K, pool, chunk + i, WH, i, hi_done, lo_done)

            @block.vector
            def _(dve):
                for i, (up, r) in enumerate(order):
                    if up:
                        for j in range(4):
                            u = 4 * r + j
                            (hi, lo), x = hidden(r, j), whole(r, j)
                            dve.wait_ge(relu_done, u + 1)
                            dve.tensor_tensor(x, x, x, ALU.mult).then_inc(sq_done, 1)
                            dve.wait_ge(sq_done, u + 1)
                            dve.tensor_copy(hi, x).then_inc(high_done, 1)
                            dve.wait_ge(high_done, u + 1)
                            dve.tensor_tensor(lo, x, hi.bitcast(F32), ALU.subtract).then_inc(low_done, 1)
                    else:
                        for t, n in TILES:
                            for half in range(2):
                                v = (r * TT + t) * 2 + half
                                dve.wait_ge(down_mm, v + 1)
                                acc, ps = ACC[0:n, t, half * 512:(half + 1) * 512], K.PS[0:n, 4 + v % 4, :]
                                if r == 0:
                                    dve.tensor_copy(acc, ps).then_inc(acc_done, 1)
                                else:
                                    dve.wait_ge(acc_done, v + 1 - 2 * TT)
                                    dve.tensor_tensor(acc, acc, ps, ALU.add).then_inc(acc_done, 1)

        with stage(nc, "sq_done", "rs_link", "rs_done", "scaled", "zeroed", "x_done") as (
                block, sq_done, rs_link, rs_done, scaled, zeroed, x_done):
            @block.sync
            def _(sp):
                if out:
                    for t in range(NT):
                        sp.wait_ge(x_done, t + 1)
                        sp.dma_start(out[0][t * P:(t + 1) * P, :], K.X[:, t, :]).then_inc(K.state_out, 16)
                    sp.wait_ge(x_done, TT)
                    sp.dma_start(out[1], K.X[0:TS, NT, :]).then_inc(K.state_out, 16)
                    K.n_state_out += TT

            @block.gpsimd
            def _(pool):
                pool.memset(ss[:], 1.0).then_inc(zeroed, 1)

            @block.scalar
            def _(act):
                act.wait_ge(zeroed, 1)
                for t, n in TILES:
                    if t:
                        act.wait_ge(sq_done, t)
                    act.activation(K.PSF[0:n, 0:D], ACC[0:n, t, :], ACT.Square, accum_out=ss[0:n, t:t + 1]).then_inc(sq_done, 1)
                inv_rms(act, K, ss[:], D, sq_done, TT, rs_link).then_inc(rs_done, 1)

            @block.vector
            def _(dve):
                dve.wait_ge(rs_done, 1)
                dve.wait_ge(K.weights_in, 16 * K.n_weights_in)
                for t, n in TILES:
                    dve.scalar_tensor_tensor(ACC[0:n, t, :], ACC[0:n, t, :], ss[0:n, t:t + 1], PW[0:n, :], ALU.mult,
                                             ALU.mult).then_inc(scaled, 1)
                    dve.wait_ge(scaled, t + 1)
                    dve.tensor_tensor(K.X[0:n, t, :], K.X[0:n, t, :], ACC[0:n, t, :], ALU.add).then_inc(x_done, 1)



def gdn(nc, K, chunk):
    with ExitStack() as ctx:
        def sb(name, shape):
            return ctx.enter_context(nc.sbuf_tensor(name, shape, F32))

        C = Ctx()
        C.beta, C.gcum, C.dl, C.beg, C.g = (sb(f"g_{n}", [P, TT, GH]) for n in ("beta", "gc", "dl", "beg", "g"))
        C.nw = sb("g_nw", [P, 1])
        gdn_scalars(nc, K, chunk, C)
        project(nc, K, "gdnz", [(chunk + 1 + c, "T", m, 512, "act",
                                 lambda act, pair, at, c=c: act.activation(
                                     in_halves(K.YT[:, 4 * c + at, 0:TOK]), both_halves(K, pair), ACT.Silu))
                                for c in range(2) for m in range(4)])
        high = K.YT[:, 8:16, :].rearrange("p k n -> p (k n)")
        HH = GH // 2
        for p in range(2):
            with ExitStack() as c2:
                SX = c2.enter_context(nc.sbuf_tensor(f"g_SX{p}", [P, 3 * HH, TP], F32))
                cols = [(i * 512, i * GW + p * 512, 512) for i in range(3)]
                with ExitStack() as c3:
                    hist = c3.enter_context(nc.sbuf_tensor(f"g_hist{p}", [P, 12, NB, CONVK - 1], F32))
                    wT = c3.enter_context(nc.sbuf_tensor(f"g_wT{p}", [P, 12, CONVK], F32))
                    keep = c3.enter_context(nc.sbuf_tensor(f"g_keep{p}", [P, 12, 27], F32))
                    K.conv_rows = high
                    conv_inputs(nc, K, 1536, 12, K.gdn_conv[0], K.gdn_conv_w[0], None, hist, wT, cols, high)
                    project_conv(nc, K, f"gconv{p}", chunk + 3 + 3 * p, 12, hist, wT, False, SX, keep, high)
                    write_conv_state(nc, K, 12, keep, K.o_gdn_conv_p[0], K.o_gdn_conv_s[0], cols)
                gdn_l2norm(nc, K, SX, high, 2 * HH, HH)
                for q in range(HH // 2):
                    gdn_pair(nc, K, C, SX, high, (2 * q, 2 * q + 1), HH * p)
                gdn_norm(nc, K, C, SX, high, HH, HH * p)


def gdn_scalars(nc, K, chunk, C):
    U = TT * GH
    with ExitStack() as ctx:
        def sb(name, shape):
            return ctx.enter_context(nc.sbuf_tensor(name, shape, F32))

        sm = [sb(f"h_sm{i}", [P, U]) for i in range(3)]
        rowp = sb("h_rowp", [P, 2, GH])
        eg = sb("h_eg", [P, U])
        gf, gcf, dlf, bef, betaf = (x[:].rearrange("p t h -> p (t h)") for x in (C.g, C.gcum, C.dl, C.beg, C.beta))
        with stage(nc, "rows_in", "ba_mm", "exp_in", "exp_out", "g_ready", "cum_mm", "cum_out", "dve_link") as (
                block, rows_in, ba_mm, exp_in, exp_out, g_ready, cum_mm, cum_out, dve_link):
            @block.sync
            def _(sp):
                fill_ring(K, sp, chunk + RING, ba_mm, {chunk: 1})

            @block.scalar
            def _(act):
                act.dma_start(rowp[:, 0, :], K.gdn_a_log[0].partition_broadcast(P)).then_inc(rows_in, 16)
                act.dma_start(rowp[:, 1, :], K.gdn_dt_bias[0].partition_broadcast(P)).then_inc(rows_in, 16)
                act.dma_start(C.nw[:], K.gdn_norm_w[0].unsqueeze(1), allow_slow_non_contiguous=True).then_inc(rows_in, 16)
                act.wait_ge(ba_mm, 1)
                act.activation(C.beta[:], K.PS[:, 0, 0:2 * U].rearrange("p (t c) -> p t c", t=TT)[:, :, 0:GH],
                               ACT.Sigmoid).then_inc(exp_out, 1)
                act.wait_ge(rows_in, 48)
                act.activation(rowp[:, 0, :], rowp[:, 0, :], ACT.Exp).then_inc(exp_out, 1)
                act.wait_ge(exp_in, 1)
                act.activation(sm[0][:], sm[0][:], ACT.Exp, scale=-1.0).then_inc(exp_out, 1)
                act.wait_ge(cum_out, 1)
                act.activation(dlf, dlf, ACT.Exp).then_inc(exp_out, 1)
                act.activation(eg[:], gcf, ACT.Exp).then_inc(exp_out, 1)

            @block.tensor
            def _(pe):
                W = chunk_wait(K, pe, chunk)
                for t in range(TT):
                    for k in range(KT):
                        last = pe.matmul(K.PS[:, 0, t * 16:(t + 1) * 16], K.HT[:, k, t * P:(t + 1) * P],
                                         W[:, k, 0:16], start=(k == 0), stop=(k == KT - 1))
                last.then_inc(ba_mm, 1)
                pe.wait_ge(g_ready, 1)
                for t in range(TT):
                    pe.matmul(K.PS[:, 1, t * GH:(t + 1) * GH], K.U5[:, t, :], C.g[:, t, :], start=True, stop=True)
                    last = pe.matmul(K.PS[:, 2, t * GH:(t + 1) * GH], K.ones[:] if t < NT else K.B8[:], C.g[:, t, :],
                                     start=True, stop=True)
                last.then_inc(cum_mm, 1)

            @block.vector
            def _(dve):
                do = Chain(dve, dve_link)
                dve.wait_ge(exp_out, 2)
                do(dve.tensor_tensor(C.g[:], K.PS[:, 0, 0:2 * U].rearrange("p (t c) -> p t c", t=TT)[:, :, GH:],
                                     bc(rowp[:, 1, :], 1, TT), ALU.add))
                dve.scalar_tensor_tensor(sm[0][:], gf, -1.0, gf, ALU.mult, ALU.max).then_inc(exp_in, 1)
                dve.wait_ge(exp_out, 3)
                log1p_series(do, dve, gf, sm[0][:], sm[1][:], sm[2][:])
                do(dve.tensor_tensor(C.g[:], C.g[:], bc(rowp[:, 0, :], 1, TT), ALU.mult))
                dve.tensor_scalar(gf, gf, -1.0, None, ALU.mult).then_inc(g_ready, 1)
                dve.wait_ge(cum_mm, 1)
                do(dve.tensor_copy(gcf, K.PS[:, 1, 0:U]))
                dve.tensor_tensor(dlf, K.PS[:, 2, 0:U], gcf, ALU.subtract).then_inc(cum_out, 1)
                dve.wait_ge(exp_out, 5)
                dve.tensor_tensor(bef, betaf, eg[:], ALU.mult)


def norm_over_partitions(nc, K, tiles, high, scale, apply):
    N = len(tiles)
    SQ = high[:, 0:2 * TOK].rearrange("p (s n) -> p s n", s=2)
    RS = high[:, 2 * TOK:4 * TOK].rearrange("p (s n) -> p s n", s=2)
    with stage(nc, "squared", "summed", "logged", "rs_ready", "used") as (block, squared, summed, logged, rs_ready, used):
        @block.tensor
        def _(pe):
            for i in range(N):
                pe.wait_ge(squared, i + 1)
                if i >= 4:
                    pe.wait_ge(logged, i - 3)
                o = (i % 4) * 1024
                pe.matmul(K.PSF[:, o:o + SEQ], K.ones[:], SQ[:, i % 2, 0:SEQ], start=True, stop=True)
                pe.matmul(K.PSF[:, o + SEQ:o + TOK], K.ones[:], SQ[:, i % 2, SEQ:TOK], start=True, stop=True).then_inc(summed, 1)

        @block.scalar
        def _(act):
            for i in range(N + 1):
                if i < N:
                    if i >= 2:
                        act.wait_ge(summed, i - 1)
                    act.activation(SQ[:, i % 2, :], tiles[i], ACT.Square).then_inc(squared, 1)
                if i >= 1:
                    j = i - 1
                    rs = RS[:, j % 2, :]
                    act.wait_ge(summed, j + 1)
                    if j >= 2:
                        act.wait_ge(used, j - 1)
                    act.activation(rs, K.PSF[:, (j % 4) * 1024:(j % 4) * 1024 + TOK], ACT.Ln, scale=scale,
                                   bias=K.eps[:]).then_inc(logged, 1)
                    act.wait_ge(logged, j + 1)
                    act.activation(rs, rs, ACT.Exp, scale=-0.5).then_inc(rs_ready, 1)

        @block.vector
        def _(dve):
            for i in range(N):
                dve.wait_ge(rs_ready, i + 1)
                apply(dve, i, RS[:, i % 2, :]).then_inc(used, 1)


def gdn_l2norm(nc, K, SX, high, n, n_q):
    tiles = [SX[:, i, 0:TOK] for i in range(n)]
    norm_over_partitions(nc, K, tiles, high, 1.0, lambda dve, i, rs: dve.scalar_tensor_tensor(
        tiles[i], tiles[i], P ** -0.5 if i < n_q else 1.0, rs, ALU.mult, ALU.mult))


def gdn_norm(nc, K, C, SX, high, n, h0):
    tiles = [SX[:, i, 0:TOK] for i in range(n)]
    with ExitStack() as ctx:
        link = ctx.enter_context(nc.semaphore(f"norm_link{h0}"))

        def apply(dve, i, rs):
            dve.tensor_tensor(tiles[i], tiles[i], rs, ALU.mult).then_inc(link, 1)
            dve.wait_ge(link, i + 1)
            y = K.YT[:, h0 + i, 0:TOK]
            return dve.scalar_tensor_tensor(y, tiles[i], C.nw[:, 0:1], y, ALU.mult, ALU.mult)
        norm_over_partitions(nc, K, tiles, high, 1.0 / P, apply)


LEVELS = 7


def gdn_pair(nc, K, C, SX, high, heads, h_base):
    with ExitStack() as ctx:
        def sb(name, shape):
            return ctx.enter_context(nc.sbuf_tensor(f"{name}_{h_base + heads[0]}", shape, F32))

        B = []
        for a in range(2):
            b = Ctx()
            if a == 0:
                big = high[:, 0:8 * TP].rearrange("p (s n) -> p s n", s=8)
            else:
                big = sb("k_big", [P, 8, TP])[:]
            tiles = [big[:, i, :] for i in range(8)]
            b.XS, b.AL, b.TM, b.E, b.DT, b.LT, b.QKD, b.TT = tiles
            b.VNm = big[0:TS, 0:2, :].rearrange("p s n -> p (s n)")[:, 0:NB * P].rearrange("p (b n) -> p b n", b=NB)
            b.VN4 = big[0:TS, 0:2, :].rearrange("p s n -> p (s n)")[:, NB * P:(NB + 1) * P]
            b.kbg = sb(f"k_kbg{a}", [P, TP])[:]
            b.S = sb(f"k_S{a}", [P, P])[:]
            b.S0 = sb(f"k_S0{a}", [P, NB, P])[:]
            h = heads[a]
            b.q, b.k, b.v = SX[:, h, :], SX[:, 4 + h, :], SX[:, 8 + h, :]
            b.kdec, b.vb, b.w, b.qg, b.O = b.k, b.v, b.LT, b.DT, b.q
            b.h = h_base + h
            b.bank = 4 * a
            b.A = K.PSF[:, 2048 * a:2048 * a + TP]
            b.Bp = K.PSF[:, 2048 * a + 1024:2048 * a + 1024 + TP]
            B.append(b)

        def t5(ap):
            return ap.rearrange("p (t n) -> p t n", n=P)

        def tile_(ap, t):
            return ap[:, t * P:(t + 1) * P]

        KS = range(1, LEVELS)
        pe_steps = (["R", "BR", "kk", "qk", "ktok", "vtok", "turnT"]
                    + [x for k in KS for x in ([("X", k), ("TX", k), ("TXT", k)] if k < LEVELS - 1 else [("X", k), ("TXT", k)])]
                    + ["w"] + [x for t in range(NT) for x in (("vn", t), ("s", t))] + ["svn", "svt", "so", "ss"])
        act_steps = (["E", "DT", "TM"] + [("XS", k) for k in KS] + ["w"] + [("VN", t) for t in range(NT)]
                     + ["VT", "VN4", "O"])
        dve_steps = (["DT", "LT1", "LT", "QKD", "TT0", "tok"]
                     + [x for k in KS for x in ([("TM", k), ("TT", k)] if k < LEVELS - 1 else [("TT", k)])]
                     + [("S", t) for t in range(NT)] + ["VNm", "S0"])
        pool_steps = ["UG", "IB"] + [("AL", k) for k in KS] + ["qg"]
        at = [{s: i + 1 for i, s in enumerate(steps)} for steps in (pe_steps, act_steps, dve_steps, pool_steps)]
        PE, AC, DV, PO = at
        with stage(nc, "pe_0", "pe_1", "act_0", "act_1", "dve_0", "dve_1", "pool_0", "pool_1", "s0_in", "dve_link") as (
                block, pe0, pe1, act0, act1, dve0, dve1, pool0, pool1, s0_in, dve_link):
            pes, acts, dves, pools = (pe0, pe1), (act0, act1), (dve0, dve1), (pool0, pool1)

            @block.sync
            def _(sp):
                for b in B:
                    sp.dma_start(b.S0, K.state_gdn[0, :, b.h].rearrange("b k v -> k b v")).then_inc(s0_in, 16)
                for a, b in enumerate(B):
                    sp.wait_ge(dves[a], DV[("S", NT - 1)])
                    sp.dma_start(K.o_gdn_p[0, 0, b.h], b.S).then_inc(K.state_out, 16)
                for a, b in enumerate(B):
                    sp.wait_ge(dves[a], DV["S0"])
                    sp.dma_start(K.o_gdn_s[0, :, b.h].rearrange("b k v -> k b v"), b.S0).then_inc(K.state_out, 16)
                K.n_state_out += 4
                sp.wait_ge(K.state_out, 16 * K.n_state_out)

            @block.gpsimd
            def _(pool):
                for a, b in enumerate(B):
                    pool.tensor_tensor(t5(b.XS), K.U5, bc(C.g[:, :, b.h], 2, P), ALU.mult).then_inc(pools[a], 1)
                    pool.tensor_tensor(t5(b.TM), bc(K.ident[:], 1, TT), bc(C.beta[:, :, b.h], 2, P),
                                       ALU.mult).then_inc(pools[a], 1)
                for k in KS:
                    for a, b in enumerate(B):
                        pool.wait_ge(dves[a], DV["LT"])
                        if k > 1:
                            pool.wait_ge(pes[a], PE[("X", k - 1)])
                        pool.tensor_tensor(t5(b.AL), t5(b.LT), bc(K.LV[:, k, :], 1, TT), ALU.mult).then_inc(pools[a], 1)
                for a, b in enumerate(B):
                    pool.wait_ge(dves[a], DV["QKD"])
                    pool.tensor_tensor(b.qg, b.q, b.E, ALU.mult).then_inc(pools[a], 1)

            @block.scalar
            def _(act):
                for a, b in enumerate(B):
                    act.wait_ge(dves[a], DV["DT"])
                    act.activation(b.E, b.A, ACT.Exp).then_inc(acts[a], 1)
                    act.activation(b.DT, b.DT, ACT.Exp).then_inc(acts[a], 1)
                for a, b in enumerate(B):
                    act.wait_ge(pes[a], PE["turnT"])
                    act.copy(b.TM, b.A).then_inc(acts[a], 1)
                for k in KS:
                    for a, b in enumerate(B):
                        n = TP if k < 3 else SEQ
                        act.wait_ge(pes[a], PE[("X", k)])
                        if k > 1:
                            act.wait_ge(pes[a], PE[("TXT", k - 1)])
                        act.copy(b.XS[:, 0:n], b.A[:, 0:n]).then_inc(acts[a], 1)
                for a, b in enumerate(B):
                    act.wait_ge(pes[a], PE["w"])
                    act.mul(b.w, b.A, -1.0).then_inc(acts[a], 1)
                for t in range(NT):
                    for a, b in enumerate(B):
                        act.wait_ge(pes[a], PE[("vn", t)])
                        act.copy(tile_(b.TM, t), tile_(b.A, t)).then_inc(acts[a], 1)
                o = 1536
                for a, b in enumerate(B):
                    f = K.PSF[:, 2048 * a + o:2048 * a + o + 512]
                    act.wait_ge(pes[a], PE["svn"])
                    act.copy(b.TM[:, SEQ:TOK], f[:, 0:TS]).then_inc(acts[a], 1)
                for a, b in enumerate(B):
                    f = K.PSF[:, 2048 * a + o:2048 * a + o + 512]
                    act.wait_ge(pes[a], PE["svt"])
                    act.copy(b.VN4, f[0:TS, P:2 * P]).then_inc(acts[a], 1)
                for a, b in enumerate(B):
                    f = K.PSF[:, 2048 * a + o:2048 * a + o + 512]
                    act.wait_ge(pes[a], PE["so"])
                    act.wait_ge(pools[a], PO["qg"])
                    act.copy(b.O[:, 0:SEQ], b.Bp[:, 0:SEQ])
                    act.copy(b.O[:, SEQ:TOK], f[:, 256:256 + TS]).then_inc(acts[a], 1)

            @block.vector
            def _(dve):
                do = Chain(dve, dve_link)
                for a, b in enumerate(B):
                    dve.wait_ge(pes[a], PE["R"])
                    do(dve.tensor_tensor(t5(b.DT), t5(b.A), bc(C.gcum[:, :, b.h], 2, P), ALU.subtract))
                    dve.tensor_tensor(t5(b.DT), t5(b.DT), K.NM5, ALU.add).then_inc(dves[a], 1)
                for a, b in enumerate(B):
                    dve.wait_ge(acts[a], AC["DT"])
                    dve.wait_ge(pes[a], PE["BR"])
                    dve.tensor_tensor(b.LT, b.Bp, b.DT, ALU.mult).then_inc(dves[a], 1)
                    dve.wait_ge(dves[a], DV["LT1"])
                    dve.wait_ge(pes[a], PE["kk"])
                    dve.tensor_tensor(b.LT, b.LT, b.A, ALU.mult).then_inc(dves[a], 1)
                for a, b in enumerate(B):
                    dve.wait_ge(pes[a], PE["qk"])
                    dve.tensor_tensor(b.QKD, b.Bp, b.DT, ALU.mult).then_inc(dves[a], 1)
                for a, b in enumerate(B):
                    do(dve.tensor_tensor(t5(b.TT), t5(b.LT), bc(K.LV[:, 0, :], 1, TT), ALU.mult))
                    dve.tensor_tensor(t5(b.TT), bc(K.ident[:], 1, TT), t5(b.TT), ALU.subtract).then_inc(dves[a], 1)
                for a, b in enumerate(B):
                    dve.wait_ge(pes[a], PE["ktok"])
                    dve.tensor_tensor(t5(b.kbg), t5(b.A), bc(C.beg[:, :, b.h], 2, P), ALU.mult)
                    dve.tensor_tensor(t5(b.kdec), t5(b.A), bc(C.dl[:, :, b.h], 2, P), ALU.mult)
                    dve.wait_ge(pes[a], PE["vtok"])
                    dve.tensor_tensor(t5(b.vb), t5(b.Bp), bc(C.beta[:, :, b.h], 2, P), ALU.mult).then_inc(dves[a], 1)
                for k in KS:
                    n = TP if k < 3 else SEQ
                    for a, b in enumerate(B):
                        if k < LEVELS - 1:
                            dve.wait_ge(pes[a], PE[("TX", k)])
                            dve.tensor_tensor(b.TM[:, 0:n], b.TM[:, 0:n], b.Bp[:, 0:n], ALU.subtract).then_inc(dves[a], 1)
                    for a, b in enumerate(B):
                        dve.wait_ge(pes[a], PE[("TXT", k)])
                        dve.tensor_tensor(b.TT[:, 0:n], b.TT[:, 0:n], b.A[:, 0:n], ALU.subtract).then_inc(dves[a], 1)
                for t in range(NT):
                    for a, b in enumerate(B):
                        p = K.PS[:, b.bank + 1, t * P:(t + 1) * P]
                        dve.wait_ge(pes[a], PE[("s", t)])
                        if t == 0:
                            dve.tensor_copy(b.S, p).then_inc(dves[a], 1)
                        else:
                            dve.scalar_tensor_tensor(b.S, b.S, b.E[:, t * P + P - 1:t * P + P], p, ALU.mult,
                                                     ALU.add).then_inc(dves[a], 1)
                for a, b in enumerate(B):
                    dve.wait_ge(acts[a], AC["VN4"])
                    dve.tensor_tensor(b.VNm, bc(b.VN4, 1, NB), bc(K.SELT[0:TS, :], 2, P), ALU.mult).then_inc(dves[a], 1)
                for a, b in enumerate(B):
                    dve.wait_ge(pes[a], PE["so"])
                    do(dve.tensor_tensor(b.S0, b.S0, bc(b.E[:, SEQ + NS - 1:TOK:NS], 2, P), ALU.mult))
                for a, b in enumerate(B):
                    dve.wait_ge(pes[a], PE["ss"])
                    dve.tensor_tensor(b.S0, b.S0, K.PSF[:, 2048 * a:2048 * a + NB * P].rearrange("p (b n) -> p b n", b=NB),
                                      ALU.add).then_inc(dves[a], 1)

            @block.tensor
            def _(pe):
                def wide(a, out, lhs, rhs):
                    pe.matmul(out[:, 0:SEQ], lhs, rhs[:, 0:SEQ], start=True, stop=True)
                    return pe.matmul(out[:, SEQ:TP], lhs, rhs[:, SEQ:TP], start=True, stop=True)

                def tiles(out, lhs, rhs, n=TT):
                    for t in range(n):
                        last = pe.matmul(tile_(out, t), tile_(lhs, t), tile_(rhs, t), start=True, stop=True)
                    return last

                def turn(out, src):
                    for t in range(TT):
                        last = pe.transpose(tile_(out, t), tile_(src, t), K.ident[:])
                    return last

                for a, b in enumerate(B):
                    pe.wait_ge(pools[a], PO["UG"])
                    wide(a, b.A, K.ones[:], b.XS).then_inc(pes[a], 1)
                    pe.wait_ge(pools[a], PO["IB"])
                    wide(a, b.Bp, K.ones[:], b.TM).then_inc(pes[a], 1)
                for a, b in enumerate(B):
                    pe.wait_ge(acts[a], AC["E"])
                    tiles(b.A, b.k, b.k).then_inc(pes[a], 1)
                for a, b in enumerate(B):
                    pe.wait_ge(dves[a], DV["LT1"])
                    tiles(b.Bp, b.k, b.q).then_inc(pes[a], 1)
                for a, b in enumerate(B):
                    pe.wait_ge(dves[a], DV["LT"])
                    turn(b.A, b.k).then_inc(pes[a], 1)
                    pe.wait_ge(dves[a], DV["QKD"])
                    turn(b.Bp, b.v).then_inc(pes[a], 1)
                for a, b in enumerate(B):
                    pe.wait_ge(dves[a], DV["tok"])
                    turn(b.A, b.TT).then_inc(pes[a], 1)
                for k in KS:
                    n = TT if k < 3 else NT
                    for a, b in enumerate(B):
                        pe.wait_ge(pools[a], PO[("AL", k)])
                        if k == 1:
                            pe.wait_ge(acts[a], AC["TM"])
                        else:
                            pe.wait_ge(dves[a], DV[("TT", k - 1)])
                        tiles(b.A, b.AL, b.TM, n).then_inc(pes[a], 1)
                    for a, b in enumerate(B):
                        pe.wait_ge(acts[a], AC[("XS", k)])
                        if k < LEVELS - 1:
                            tiles(b.Bp, b.TT, b.XS, n).then_inc(pes[a], 1)
                    for a, b in enumerate(B):
                        tiles(b.A, b.XS, b.TT, n).then_inc(pes[a], 1)
                for a, b in enumerate(B):
                    pe.wait_ge(dves[a], DV[("TT", LEVELS - 1)])
                    tiles(b.A, b.kbg, b.TT).then_inc(pes[a], 1)
                for t in range(NT):
                    for a, b in enumerate(B):
                        out = tile_(b.A, t)
                        if t == 0:
                            pe.wait_ge(acts[a], AC["w"])
                            pe.wait_ge(pools[a], PO["qg"])
                        vn = pe.matmul(out, tile_(b.TT, t), tile_(b.vb, t), start=True, stop=(t == 0))
                        if t:
                            pe.wait_ge(dves[a], DV[("S", t - 1)])
                            vn = pe.matmul(out, tile_(b.w, t), b.S, start=False, stop=True)
                        vn.then_inc(pes[a], 1)
                    for a, b in enumerate(B):
                        pe.wait_ge(acts[a], AC[("VN", t)])
                        o = tile_(b.Bp, t)
                        pe.matmul(o, tile_(b.TM, t), tile_(b.QKD, t), start=True, stop=(t == 0))
                        if t:
                            pe.matmul(o, b.S, tile_(b.qg, t), start=False, stop=True)
                        pe.matmul(K.PS[:, b.bank + 1, t * P:(t + 1) * P], tile_(b.kdec, t), tile_(b.TM, t),
                                  start=True, stop=True).then_inc(pes[a], 1)
                pe.wait_ge(s0_in, 32)
                for a, b in enumerate(B):
                    out = K.PS[:, b.bank + 3, 0:TS]
                    pe.matmul(out, b.vb[0:TS, SEQ:TP], b.TT[0:TS, SEQ:TOK], start=True, stop=False, skip_group_check=True)
                    for s in range(NB):
                        last = pe.matmul(out[:, s * NS:(s + 1) * NS], b.S0[:, s, :], b.w[:, SEQ + s * NS:SEQ + (s + 1) * NS],
                                         start=False, stop=(s == NB - 1), skip_group_check=True)
                    last.then_inc(pes[a], 1)
                for a, b in enumerate(B):
                    pe.wait_ge(acts[a], AC["VT"])
                    pe.transpose(K.PS[0:TS, b.bank + 3, P:2 * P], b.TM[:, SEQ:TOK], K.ident[:]).then_inc(pes[a], 1)
                for a, b in enumerate(B):
                    pe.wait_ge(acts[a], AC["VN4"])
                    out = K.PS[:, b.bank + 3, 256:256 + TS]
                    pe.matmul(out, b.VN4, b.QKD[0:TS, SEQ:TOK], start=True, stop=False, skip_group_check=True)
                    for s in range(NB):
                        last = pe.matmul(out[:, s * NS:(s + 1) * NS], b.S0[:, s, :], b.qg[:, SEQ + s * NS:SEQ + (s + 1) * NS],
                                         start=False, stop=(s == NB - 1), skip_group_check=True)
                    last.then_inc(pes[a], 1)
                for a, b in enumerate(B):
                    pe.wait_ge(dves[a], DV["VNm"])
                    for half in range(2):
                        last = pe.matmul(K.PS[:, b.bank + half, :], b.kdec[0:TS, SEQ:TP], b.VNm[:, 4 * half:4 * half + 4, :],
                                         start=True, stop=True)
                    last.then_inc(pes[a], 1)



DG = 3
DIL_W = (128, 512, 2048)


def dilated(nc, K, chunk):
    HP = DH // 2
    with ExitStack() as ctx:
        def sb(name, shape):
            return ctx.enter_context(nc.sbuf_tensor(name, shape, F32))

        K.MS = sb("MS", [P, P + 2 * PAST])
        K.HM = sb("HM", [P, HP, DH])
        dilated_masks(nc, K)
        QA = sb("d_Q", [P, 2 * HP, TOK])
        q_tiles = [QA[:, i, :] for i in range(2 * HP)] + [K.YT[:, 12 + i, 0:TOK] for i in range(HP)]
        KD = sb("d_K", [P, DG * HP, TOK])
        V = sb("d_V", [P, TT, DG * DW])
        spare = sb("d_spare", [P, 1280])
        KST = spare[:, 0:2 * DW].rearrange("p (s n) -> p s n", s=2)

        def q_out(c):
            def evac(eng, pair, at):
                return copy_on(eng, in_halves(q_tiles[HP * c + at]), both_halves(K, pair))
            return evac
        project(nc, K, "dilq", [(chunk + c, "T", m, 512, ("act", "dve")[m % 2], q_out(c)) for c in range(DG) for m in range(HP)])
        dilated_keys(nc, K, chunk + DG, KD, KST)

        def v_out(c):
            def evac(eng, pair, t):
                n = TILES[t][1]
                return copy_on(eng, V[0:n, t, c * DW:(c + 1) * DW], K.PSF[0:n, pair * 1024:pair * 1024 + DW])
            return evac
        project(nc, K, "dilv", [(chunk + 2 * DG + c, "N", t, 512, ("act", "dve")[t % 2], v_out(c))
                                for c in range(DG) for t in range(TT)])
        dilated_prompt_heads(nc, K, q_tiles, KD, V, spare)
        dilated_sample(nc, K, q_tiles, KD, V, spare)


def dilated_keys(nc, K, chunk, KD, KST):
    units = [(c, t) for c in range(DG) for t in range(TT)]
    with stage(nc, "k_mm", "k_rows", "turned", "k_copied") as (block, k_mm, k_rows, turned, k_copied):
        stores = []
        for c, t in units:
            if t < NT:
                o = K.o_dil_p[c][0, 0, :, 0].rearrange("s h d -> s (h d)")
                w = min(DIL_W[c], SEQ)
                at = t * P - (SEQ - w)
                stores.append([(o[at:at + P], 0, P)] if at >= 0 else [])
            else:
                w = min(DIL_W[c], PAST)
                stores.append([(K.o_dil_s[c][0, b, w - NS:, 0].rearrange("s h d -> s (h d)"), b * NS, NS) for b in range(NB)])

        @block.sync
        def _(sp):
            fill_ring(K, sp, chunk + 2)
            for i, (c, t) in enumerate(units):
                sp.wait_ge(k_rows, i + 1)
                for dst, p0, n in stores[i]:
                    sp.dma_start(dst, KST[p0:p0 + n, i % 2, :]).then_inc(K.keys_out[i % 2], 16)
                    K.n_keys_out[i % 2] += 1
                if t == TT - 1:
                    fill_ring(K, sp, chunk + c + RING, k_mm, {chunk + e: TT * (e + 1) for e in range(DG)})

        @block.tensor
        def _(pe):
            def turn(i):
                n = TILES[units[i][1]][1]
                pe.wait_ge(k_rows, i + 1)
                if i >= 2:
                    pe.wait_ge(k_copied, i - 1)
                for h in range(DH // 2):
                    last = pe.transpose(K.PS[:, 4 + i % 2, h * P:h * P + n], KST[0:n, i % 2, h * P:(h + 1) * P], K.ident[0:n, 0:n])
                last.then_inc(turned, 1)

            for i, (c, t) in enumerate(units):
                if t == 0:
                    W = chunk_wait(K, pe, chunk + c)
                if i >= 2:
                    pe.wait_ge(k_rows, i - 1)
                proj_matmuls(K, pe, W, "N", t, i % 2).then_inc(k_mm, 1)
                if i:
                    turn(i - 1)
            turn(len(units) - 1)

        @block.scalar
        def _(act):
            sent = [0, 0]
            for i, (c, t) in enumerate(units):
                n = TILES[t][1]
                act.wait_ge(k_mm, i + 1)
                if i >= 2:
                    act.wait_ge(turned, i - 1)
                    act.wait_ge(K.keys_out[i % 2], 16 * sent[i % 2])
                act.copy(KST[0:n, i % 2, :], K.PSF[0:n, (i % 2) * 1024:(i % 2) * 1024 + DW]).then_inc(k_rows, 1)
                sent[i % 2] += len(stores[i])

        @block.vector
        def _(dve):
            for i, (c, t) in enumerate(units):
                n = TILES[t][1]
                dve.wait_ge(turned, i + 1)
                dve.tensor_copy(KD[:, 4 * c:4 * c + 4, t * P:t * P + n],
                                K.PS[:, 4 + i % 2, :].rearrange("p (h n) -> p h n", h=4)[:, :, 0:n]).then_inc(k_copied, 1)


def dilated_prompt_heads(nc, K, q_tiles, KD, V, spare):
    units = [(h, i) for h in range(DH) for i in range(NT)]
    N = len(units)
    work = K.HT[:].rearrange("p k n -> p (k n)")
    SE = (work[:, 0:1280], work[:, 1280:2560], spare)
    PT = work[:, 2560:5120].rearrange("p (s n) -> p s n", s=2)
    with ExitStack() as ctx:
        nm = ctx.enter_context(nc.sbuf_tensor("f_nm", [P, 3], F32))
        sm = ctx.enter_context(nc.sbuf_tensor("f_sm", [P, 3], F32))

        def pieces(i):
            lo = max(0, i - 1) * P
            out = [(0, P if i == 0 else 0, lo, (i + 1) * P)]
            for g in (1, 2):
                out.append((g, 256 + 512 * (g - 1) + (NT - 1 - i) * P, 0, (i + 1) * P))
            return out

        def keys(i):
            return [(g, k) for g, _, a, b in pieces(i) for k in range(a // P, b // P)]

        with stage(nc, "s_mm", "s_read", "nm_ready", "exp_done", "r_ready", "p_ready", "turned", "t_act", "t_dve",
                   "pv_done", "y_out", "v_out", "dve_link") as (block, s_mm, s_read, nm_ready, exp_done, r_ready, p_ready,
                                                               turned, t_act, t_dve, pv_done, y_out, v_out, dve_link):
            @block.sync
            def _(sp):
                for c in range(DG):
                    w, cc = min(DIL_W[c], SEQ), slice(c * DW, (c + 1) * DW)
                    t0 = (SEQ - w) // P
                    sp.dma_start(K.o_dil_p[c][0, 0, :, 1].rearrange("(t p) h d -> p t (h d)", p=P), V[:, t0:NT, cc])\
                      .then_inc(K.state_out, 16)
                    w = min(DIL_W[c], PAST)
                    for b in range(NB):
                        sp.dma_start(K.o_dil_s[c][0, b, w - NS:, 1].rearrange("s h d -> s (h d)"),
                                     V[b * NS:(b + 1) * NS, NT, cc]).then_inc(K.state_out, 16)
                K.n_state_out += DG * (1 + NB)
                sp.wait_ge(K.state_out, 16 * K.n_state_out)

            @block.tensor
            def _(pe):
                def scores(u):
                    h, i = units[u]
                    r = slice((h % 2) * HD, (h % 2 + 1) * HD)
                    if u:
                        pe.wait_ge(s_read, u)
                    for g, _, a, b in pieces(i):
                        last = pe.matmul(K.PS[:, g, 0:b - a], q_tiles[4 * g + h // 2][r, i * P:(i + 1) * P],
                                         KD[r, 4 * g + h // 2, a:b], start=True, stop=True)
                    last.then_inc(s_mm, 1)

                def turn(u):
                    n = len(keys(units[u][1]))
                    pe.wait_ge(p_ready, u + 1)
                    if u:
                        pe.wait_ge(t_act, u)
                        pe.wait_ge(t_dve, u)
                    for k in range(n):
                        last = pe.transpose(K.PSF[:, 1536 + k * P:1536 + (k + 1) * P], SE[u % 3][:, k * P:(k + 1) * P], K.ident[:])
                    last.then_inc(turned, 1)

                def values(u):
                    h, i = units[u]
                    out = K.PS[(h % 2) * HD:(h % 2 + 1) * HD, 6 + h % 2, i * P:(i + 1) * P]
                    if i == 0 and h >= 2:
                        pe.wait_ge(y_out, h - 1)
                    pe.wait_ge(t_act, u + 1)
                    pe.wait_ge(t_dve, u + 1)
                    ks = keys(i)
                    for n, (g, k) in enumerate(ks):
                        last = pe.matmul(out, V[:, k, g * DW + h * HD:g * DW + (h + 1) * HD], PT[:, u % 2, n * P:(n + 1) * P],
                                         start=(n == 0), stop=(n == len(ks) - 1))
                    last.then_inc(pv_done, 1)

                for s in range(N + 3):
                    if s < N:
                        scores(s)
                    if 2 <= s < N + 2:
                        turn(s - 2)
                    if s >= 3:
                        values(s - 3)

            @block.scalar
            def _(act):
                def evacuate(u):
                    n = len(keys(units[u][1]))
                    m = min(n, 4) * P
                    act.wait_ge(turned, u + 1)
                    if u >= 2:
                        act.wait_ge(pv_done, u - 1)
                    act.copy(PT[:, u % 2, 0:m], K.PSF[:, 1536:1536 + m]).then_inc(t_act, 1)

                for u in range(N):
                    if u >= 3:
                        evacuate(u - 3)
                    n = len(keys(units[u][1])) * P
                    act.wait_ge(nm_ready, u + 1)
                    act.activation(SE[u % 3][:, 0:n], SE[u % 3][:, 0:n], ACT.Exp, scale=SCALE, bias=nm[:, u % 3:u % 3 + 1],
                                   accum_out=sm[:, u % 3:u % 3 + 1]).then_inc(exp_done, 1)
                for u in range(N - 3, N):
                    evacuate(u)

            @block.gpsimd
            def _(pool):
                for u in range(N):
                    n = len(keys(units[u][1])) * P
                    pool.wait_ge(r_ready, u + 1)
                    pool.tensor_scalar(SE[u % 3][:, 0:n], SE[u % 3][:, 0:n], sm[:, u % 3:u % 3 + 1], None,
                                       ALU.mult).then_inc(p_ready, 1)

            @block.vector
            def _(dve):
                do = Chain(dve, dve_link)

                def front(u):
                    h, i = units[u]
                    dve.wait_ge(s_mm, u + 1)
                    if u >= 3:
                        dve.wait_ge(turned, u - 2)
                    o = 0
                    for g, m, a, b in pieces(i):
                        last = dve.tensor_tensor(SE[u % 3][:, o:o + b - a], K.PS[:, g, 0:b - a], K.MJ[:, m:m + b - a], ALU.add)
                        o += b - a
                    last.then_inc(s_read, 1)
                    dve.wait_ge(s_read, u + 1)
                    do(dve.tensor_reduce(nm[:, u % 3:u % 3 + 1], SE[u % 3][:, 0:o], AX.X, ALU.max))
                    dve.tensor_scalar(nm[:, u % 3:u % 3 + 1], nm[:, u % 3:u % 3 + 1], -SCALE, None, ALU.mult).then_inc(nm_ready, 1)

                def back(u):
                    dve.wait_ge(exp_done, u + 1)
                    dve.reciprocal(sm[:, u % 3:u % 3 + 1], sm[:, u % 3:u % 3 + 1]).then_inc(r_ready, 1)

                def evacuate(u):
                    n = len(keys(units[u][1])) * P
                    dve.wait_ge(turned, u + 1)
                    if u >= 2:
                        dve.wait_ge(pv_done, u - 1)
                    if n > 4 * P:
                        dve.tensor_copy(PT[:, u % 2, 4 * P:n], K.PSF[:, 1536 + 4 * P:1536 + n]).then_inc(t_dve, 1)
                    else:
                        dve.engine_nop().then_inc(t_dve, 1)

                def y(h):
                    r = slice((h % 2) * HD, (h % 2 + 1) * HD)
                    dve.wait_ge(pv_done, (h + 1) * NT)
                    dve.tensor_copy(K.YT[r, 8 + h // 2, 0:SEQ], K.PS[r, 6 + h % 2, :]).then_inc(y_out, 1)

                for s in range(N + 3):
                    if s >= 3:
                        evacuate(s - 3)
                    if s < N:
                        front(s)
                    if 1 <= s <= N:
                        back(s - 1)
                    if s >= 8 and (s - 8) % NT == 0:
                        y((s - 8) // NT)
                y(DH - 1)


def dilated_sample(nc, K, q_tiles, KD, V, spare):
    HP = DH // 2
    OLD = P + 2 * PAST
    NEW = DG * TS
    R = DH * NS
    old = [K.HT[:].rearrange("p k n -> p (k n)").rearrange("p (n c) -> p n c", n=5),
           V[:, 0:NT, :].rearrange("p t c -> p (t c)")[:, 0:5120].rearrange("p (n c) -> p n c", n=5)]
    KTb = KD[:, 0:10, 0:SEQ].rearrange("p (s n) (h c) -> p s n h c", s=2, h=HP)
    E = V[0:R, 0:NT, :].rearrange("p t c -> p (t c)")[:, 5120:5120 + OLD + NEW]
    o = DG * HP * R
    PT = spare[:, o:o + 5 * R].rearrange("p (n r) -> p n r", n=5)
    PTn = spare[0:TS, o + 5 * R:o + (5 + DG) * R].rearrange("p (n r) -> p n r", n=DG)
    Qz = spare[:, 0:o].rearrange("p (g h r) -> p g h r", g=DG, h=HP)
    pattern = (0, 1, 1, 2, 2)
    with ExitStack() as ctx:
        mx = ctx.enter_context(nc.sbuf_tensor("v_mx", [R, 1], F32))
        sm = ctx.enter_context(nc.sbuf_tensor("v_sm", [R, 1], F32))
        with stage(nc, "old_even", "old_odd", "v_even", "v_odd", "k_turned", "k_copied", "q_ready", "s_mm", "nm_ready", "exp_done", "p_ready",
                   "turned", "t_copied", "pv_done", "y_out", "dve_link") as (
                block, old_even, old_odd, v_even, v_odd, k_turned, k_copied, q_ready, s_mm, nm_ready, exp_done, p_ready, turned,
                t_copied, pv_done, y_out, dve_link):
            @block.sync
            def _(sp):
                def load(b, kv, sem):
                    for c, n0 in ((0, 0), (1, 1), (2, 3)):
                        n = K.dil[c].shape[2] // P
                        sp.dma_start(old[b % 2][:, n0:n0 + n, kv * DW:(kv + 1) * DW],
                                     K.dil[c][0, b, :, kv].rearrange("(n p) h d -> p n (h d)", p=P)).then_inc(sem, 16)

                for b in range(NB + 1):
                    if b < NB:
                        if b >= 2:
                            sp.wait_ge(k_turned, 5 * (b - 1))
                        load(b, 0, (old_even, old_odd)[b % 2])
                    if b >= 1:
                        if b >= 3:
                            sp.wait_ge(pv_done, b - 2)
                        load(b - 1, 1, (v_even, v_odd)[(b - 1) % 2])

            @block.tensor
            def _(pe):
                def turn_keys(b):
                    pe.wait_ge((old_even, old_odd)[b % 2], 48 * (b // 2 + 1))
                    for n in range(5):
                        i = 5 * b + n
                        if i >= 2:
                            pe.wait_ge(k_copied, i - 1)
                        for h in range(HP):
                            last = pe.transpose(K.PS[:, i % 2, h * P:(h + 1) * P], old[b % 2][:, n, h * P:(h + 1) * P], K.ident[:])
                        last.then_inc(k_turned, 1)

                turn_keys(0)
                for b in range(NB):
                    pe.wait_ge(q_ready, b + 1)
                    pe.wait_ge(k_copied, 5 * (b + 1))
                    if b:
                        pe.wait_ge(nm_ready, b)
                    for n in range(5):
                        g = pattern[n]
                        for h in range(HP):
                            pe.matmul(K.PSF[0:R, 1024 + n * P:1024 + (n + 1) * P], Qz[:, g, h, :], KTb[:, b % 2, n, h, :],
                                      start=(h == 0), stop=(h == HP - 1))
                    for g in range(DG):
                        for h in range(HP):
                            last = pe.matmul(K.PSF[0:R, 1024 + OLD + g * TS:1024 + OLD + (g + 1) * TS], Qz[:, g, h, :],
                                             KD[:, 4 * g + h, SEQ:TOK], start=(h == 0), stop=(h == HP - 1))
                    last.then_inc(s_mm, 1)
                    if b + 1 < NB:
                        turn_keys(b + 1)
                    pe.wait_ge(p_ready, b + 1)
                    if b:
                        pe.wait_ge(t_copied, b)
                    for n in range(5):
                        pe.transpose(K.PS[:, 4, n * R:(n + 1) * R], E[:, n * P:(n + 1) * P], K.ident[0:R, 0:R])
                    for g in range(DG):
                        last = pe.transpose(K.PS[0:TS, 5, g * R:(g + 1) * R], E[:, OLD + g * TS:OLD + (g + 1) * TS], K.ident[0:R, 0:R])
                    last.then_inc(turned, 1)
                    pe.wait_ge(t_copied, b + 1)
                    pe.wait_ge((v_even, v_odd)[b % 2], 48 * (b // 2 + 1))
                    if b:
                        pe.wait_ge(y_out, b)
                    for h in range(HP):
                        out = K.PS[:, 6, h * 2 * NS:(h + 1) * 2 * NS]
                        for n in range(5):
                            pe.matmul(out, old[b % 2][:, n, DW + h * P:DW + (h + 1) * P],
                                      PT[:, n, :].rearrange("p (i h) -> p i h", h=DH)[:, :, 2 * h:2 * h + 2],
                                      start=(n == 0), stop=False)
                        for g in range(DG):
                            last = pe.matmul(out, V[0:TS, NT, g * DW + h * P:g * DW + (h + 1) * P],
                                             PTn[:, g, :].rearrange("p (i h) -> p i h", h=DH)[:, :, 2 * h:2 * h + 2],
                                             start=False, stop=(g == DG - 1))
                    last.then_inc(pv_done, 1)

            @block.scalar
            def _(act):
                def copy_keys(b):
                    for n in range(5):
                        i = 5 * b + n
                        act.wait_ge(k_turned, i + 1)
                        if b >= 2:
                            act.wait_ge(s_mm, b - 1)
                        act.copy(KTb[:, b % 2, n].rearrange("p h c -> p (h c)"), K.PS[:, i % 2, :]).then_inc(k_copied, 1)

                copy_keys(0)
                for b in range(NB):
                    if b + 1 < NB:
                        copy_keys(b + 1)
                    act.wait_ge(nm_ready, b + 1)
                    act.activation(E, E, ACT.Exp, scale=SCALE, bias=mx[:], accum_out=sm[:]).then_inc(exp_done, 1)

            @block.vector
            def _(dve):
                do = Chain(dve, dve_link)

                def queries(b):
                    t0 = SEQ + b * NS
                    for g in range(DG):
                        for h in range(HP):
                            last = dve.tensor_tensor(Qz[:, g, h, :].rearrange("p (i h) -> p i h", h=DH),
                                                     bc(q_tiles[4 * g + h][:, t0:t0 + NS], 2, DH), bc(K.HM[:, h, :], 1, NS), ALU.mult)
                    last.then_inc(q_ready, 1)

                queries(0)
                for b in range(NB):
                    t0 = SEQ + b * NS
                    dve.wait_ge(s_mm, b + 1)
                    if b:
                        dve.wait_ge(turned, b)
                    o = (7 - b) * NS
                    new = K.MO[0:R].rearrange("p g a s -> p g (a s)")[:, :, o:o + TS]
                    dve.tensor_tensor(E[:, 0:OLD], K.PSF[0:R, 1024:1024 + OLD], K.MS[0:R, :], ALU.add)
                    do(dve.tensor_tensor(E[:, OLD:].rearrange("p (g n) -> p g n", g=DG),
                                         K.PSF[0:R, 1024 + OLD:1024 + OLD + NEW].rearrange("p (g n) -> p g n", g=DG), new, ALU.add))
                    do(dve.tensor_reduce(mx[:], E, AX.X, ALU.max))
                    dve.tensor_scalar(mx[:], mx[:], -SCALE, None, ALU.mult).then_inc(nm_ready, 1)
                    if b + 1 < NB:
                        queries(b + 1)
                    dve.wait_ge(exp_done, b + 1)
                    do(dve.reciprocal(sm[:], sm[:]))
                    dve.tensor_scalar(E, E, sm[:], None, ALU.mult).then_inc(p_ready, 1)
                    dve.wait_ge(turned, b + 1)
                    if b:
                        dve.wait_ge(pv_done, b)
                    dve.tensor_copy(PT.rearrange("p n r -> p (n r)"), K.PS[:, 4, 0:5 * R])
                    dve.tensor_copy(PTn.rearrange("p n r -> p (n r)"), K.PS[0:TS, 5, 0:DG * R]).then_inc(t_copied, 1)
                    dve.wait_ge(pv_done, b + 1)
                    for e in range(2):
                        r = slice(e * HD, (e + 1) * HD)
                        last = dve.tensor_copy(K.YT[r, 8:8 + HP, t0:t0 + NS],
                                               K.PS[r, 6, 0:HP * 2 * NS].rearrange("p (h i e) -> p h i e", h=HP, e=2)[:, :, :, e])
                    last.then_inc(y_out, 1)



def build(nc, K, upto=99):
    with ExitStack() as ctx:
        def sb(name, shape, dt=F32):
            return ctx.enter_context(nc.sbuf_tensor(name, shape, dt))

        def sem(name):
            return ctx.enter_context(nc.semaphore(name))

        K.n_phys = K.nsa_kv.shape[1]
        K.PS = ctx.enter_context(nc.psum_tensor("PS", [P, 8, 512], F32))
        K.PSF = K.PS[:].rearrange("p b n -> p (b n)")
        K.X = sb("X", [P, TT, D])
        def sb2(name, shape):
            at = -(-nc.sbuf_base // 32) * 32
            return sb(name, shape), nc.alloc_sbuf_tensor_at(f"{name}r", shape, F32R, offset=at)

        K.HT, K.HTr = sb2("HT", [P, KT, TP])
        K.YT, K.YTr = sb2("YT", [P, 16, TP])
        K.WR, K.WRr = sb2("WR", [P, RING, 8, 512])
        K.eps = sb("eps", [P, 1])
        K.normT = sb("normT", [P, 4, KT])
        K.ident, K.ones, K.B8, K.CM = (sb(n, [P, P]) for n in ("ident", "ones", "B8", "CM"))
        UN = sb("UN", [P, 2 * TT * P])
        K.U5, K.NM5 = (UN[:, i * TT * P:(i + 1) * TT * P].rearrange("p (t n) -> p t n", t=TT) for i in range(2))
        K.MJ = UN[:]
        K.CV, K.CN = sb("CV", [P, NT, NBLK]), sb("CN", [P, NT, NBLK])
        K.R8, K.SELH = sb("R8", [8, P]), sb("SELH", [P, NH])
        K.SELC, K.SELT = sb("SELC", [P, NB, TS]), sb("SELT", [P, NB])
        K.MO = sb("MO", [P, 3, 15, NS])
        K.w_landed = [sem(f"w_landed{i}") for i in range(RING)]
        K.x_in, K.small_in, K.past_in, K.kept, K.state_out, K.weights_in = (
            sem(n) for n in ("x_in", "small_in", "past_in", "kept", "state_out", "weights_in"))
        K.n_weights_in = 0
        K.keys_out = [sem(f"keys_out{i}") for i in range(2)]
        K.n_state_out, K.n_keys_out = 0, [0, 0]
        K.issued = 0
        K.chunks = plan_chunks(K)
        initialise(nc, K)
        norm_transpose(nc, K, 0)
        ssm(nc, K, 0)
        nsa(nc, K, 6)
        project_out(nc, K, "mix0", 14, [8, 8], K.norm_mix_post[0])
        mlp(nc, K, 0, 18)
        norm_transpose(nc, K, 2)
        with ExitStack() as c1:
            K.LV = c1.enter_context(nc.sbuf_tensor("LV", [P, LEVELS, P], F32))
            gdn_masks(nc, K)
            gdn(nc, K, 34)
        dilated(nc, K, 43)
        project_out(nc, K, "mix1", 52, [8, 4], K.norm_mix_post[1])
        mlp(nc, K, 1, 56, (K.o_y_p[0], K.o_y_s.rearrange("b s d -> (b s) d")))
        with stage(nc, "y_done") as (block, y_done):
            @block.sync
            def _(sp):
                sp.wait_ge(K.kept, 64)
                sp.wait_ge(K.past_in, 16 * NB * PAGES)
                sp.wait_ge(K.state_out, 16 * K.n_state_out)
                for i in range(2):
                    sp.wait_ge(K.keys_out[i], 16 * K.n_keys_out[i])
                for i in range(RING):
                    sp.wait_ge(K.w_landed[i], 16 * sum(len(K.chunks[m]) for m in range(i, K.issued, RING)))



_INS = ["x_prompt", "x_sample", "cache_ssm_conv", "state_ssm", "cache_nsa_kv", "cache_nsa_win_kv", "cache_gdn_conv",
        "state_gdn", "cache_dil0_kv", "cache_dil1_kv", "cache_dil2_kv", "page_table", "norm_mix_pre", "norm_mix_post",
        "norm_mlp_pre", "norm_mlp_post", "mlp_w1", "mlp_w2", "ab_w_in", "ab_w_out", "ssm_conv_w", "ssm_conv_b",
        "ssm_dt_bias", "ssm_a_log", "ssm_d", "ssm_norm_w", "nsa_pe_k", "nsa_pe_v", "nsa_ck_w1", "nsa_ck_w2",
        "nsa_cv_w1", "nsa_cv_w2", "cd_w_in", "cd_w_out", "gdn_conv_w", "gdn_dt_bias", "gdn_a_log", "gdn_norm_w"]
_OUTS = [("y_prompt", (1, SEQ, D)), ("y_sample", (NB, NS, D)), ("ssm_conv_p", (1, 1, 3, SCONV)),
         ("ssm_conv_s", (1, NB, 3, SCONV)), ("ssm_p", (1, 1, SH, HD, P)), ("ssm_s", (1, NB, SH, HD, P)),
         ("nsa_kv_p", (1, 1, SEQ, 4, 2, HD)), ("nsa_kv_s", (1, NB, NS, 4, 2, HD)),
         ("nsa_win_p", (1, 1, SEQ, 2, 2, HD)), ("nsa_win_s", (1, NB, PAST, 2, 2, HD)),
         ("gdn_conv_p", (1, 1, 3, 3 * GW)), ("gdn_conv_s", (1, NB, 3, 3 * GW)), ("gdn_p", (1, 1, GH, P, P)),
         ("gdn_s", (1, NB, GH, P, P)), ("dil0_p", (1, 1, 128, 2, DH, HD)), ("dil0_s", (1, NB, 128, 2, DH, HD)),
         ("dil1_p", (1, 1, SEQ, 2, DH, HD)), ("dil1_s", (1, NB, PAST, 2, DH, HD)),
         ("dil2_p", (1, 1, SEQ, 2, DH, HD)), ("dil2_s", (1, NB, PAST, 2, DH, HD))]


def kernel(**inputs):
    import numpy as _np
    import concourse.bacc as _bacc
    from concourse import mybir as _mybir
    from concourse.bass_utils import run_bass_kernel_spmd as _run

    nc = _bacc.Bacc("TRN2", target_bir_lowering=False, num_devices=1, dynamic_dma_scratch_size=1024)
    arrays, i, o = {}, {}, {}
    for name in _INS:
        a = _np.ascontiguousarray(inputs[name])
        arrays[f"in_{name}"] = a
        i[name] = nc.dram_tensor(f"in_{name}", a.shape, _mybir.dt.from_np(a.dtype), kind="ExternalInput").ap()
    for name, shape in _OUTS:
        o[name] = nc.dram_tensor(f"out_{name}", shape, F32, kind="ExternalOutput").ap()
    K = Ctx()
    (K.x_prompt, K.x_sample, K.ssm_conv, K.state_ssm, K.nsa_kv, K.nsa_win, K.gdn_conv, K.state_gdn, d0, d1, d2,
     K.page_table, K.norm_mix_pre, K.norm_mix_post, K.norm_mlp_pre, K.norm_mlp_post, K.mlp_w1, K.mlp_w2, K.ab_w_in,
     K.ab_w_out, K.ssm_conv_w, K.ssm_conv_b, K.ssm_dt_bias, K.ssm_a_log, K.ssm_d, K.ssm_norm_w, K.nsa_pe_k,
     K.nsa_pe_v, K.nsa_ck_w1, K.nsa_ck_w2, K.nsa_cv_w1, K.nsa_cv_w2, K.cd_w_in, K.cd_w_out, K.gdn_conv_w,
     K.gdn_dt_bias, K.gdn_a_log, K.gdn_norm_w) = (i[n] for n in _INS)
    K.dil = (d0, d1, d2)
    (K.o_y_p, K.o_y_s, K.o_ssm_conv_p, K.o_ssm_conv_s, K.o_ssm_p, K.o_ssm_s, K.o_nsa_kv_p, K.o_nsa_kv_s,
     K.o_nsa_win_p, K.o_nsa_win_s, K.o_gdn_conv_p, K.o_gdn_conv_s, K.o_gdn_p, K.o_gdn_s, p0, s0, p1, s1, p2,
     s2) = (o[n] for n, _ in _OUTS)
    K.o_dil_p, K.o_dil_s = (p0, p1, p2), (s0, s1, s2)
    K.past = nc.dram_tensor("past_rows", (NB, PAST, 4 * 2 * HD), F32).ap()
    K.gate_rows = nc.dram_tensor("gate_rows", (TS, 3 * NH), F32).ap()
    build(nc, K)
    r = _run(nc, [arrays], core_ids=[0])
    return tuple(r.results[0][f"out_{name}"] for name, _ in _OUTS)
```
